# Optimizing a Trainium2 kernel written in Bass

```python
import jax, jax.numpy as jnp
from jax import lax
import numpy as np

D_MODEL = 1024
BATCH = 1
SEQ = 1024
DEPTH = 2

CHUNK = 64
N_A_LAYERS = DEPTH // 2
N_B_LAYERS = DEPTH - N_A_LAYERS
HG_HEADS = 8
HG_EXPAND = 128
HG_F_DIM = HG_HEADS * HG_EXPAND
HG_V_DIM = D_MODEL
HG_HEAD_V = HG_V_DIM // HG_HEADS
HG_IN_DIM = 2 * HG_F_DIM + 2 * HG_V_DIM
SW_Q_HEADS = 16
SW_KV_HEADS = 4
SW_HEAD_DIM = D_MODEL // SW_Q_HEADS
SW_GROUP = SW_Q_HEADS // SW_KV_HEADS
SW_KV_DIM = SW_KV_HEADS * SW_HEAD_DIM
WINDOW = 128
WINDOW_CHUNKS = WINDOW // CHUNK
D_FF = 4 * D_MODEL
EPS = 1e-6

kernel_name = "hgrn2_yoco_swa_sink_hybrid"

def _rmsnorm(x, gain):
    xf = x.astype(jnp.float32)
    y = xf * lax.rsqrt(jnp.mean(xf * xf, axis=-1, keepdims=True) + EPS)
    return (y * gain.astype(jnp.float32)).astype(x.dtype)

def _modulate(h, shift, scale):
    return h * (1 + scale[:, None, :]) + shift[:, None, :]

def _hgrn2_chunk_scan(q, k, v, log_f):
    B, T, H, DK = q.shape
    DV = v.shape[-1]
    nc = T // CHUNK

    def to_chunks(a):
        return a.reshape(B, nc, CHUNK, H, a.shape[-1]).transpose(1, 0, 3, 2, 4)

    qc, kc, vc, gc = to_chunks(q), to_chunks(k), to_chunks(v), to_chunks(log_f)
    causal = jnp.tril(jnp.ones((CHUNK, CHUNK), dtype=bool))

    def step(S, inp):
        q_, k_, v_, g_ = inp
        b = jnp.cumsum(g_, axis=2)
        o_inter = jnp.einsum('bhtk,bhkv->bhtv', q_ * jnp.exp(b), S)
        diff = b[:, :, :, None, :] - b[:, :, None, :, :]
        decay = jnp.exp(jnp.where(causal[:, :, None], diff, -jnp.inf))
        scores = jnp.einsum('bhtk,bhsk,bhtsk->bhts', q_, k_, decay)
        o_intra = jnp.einsum('bhts,bhsv->bhtv', scores, v_)
        b_last = b[:, :, -1, :]
        S = jnp.exp(b_last)[..., None] * S + jnp.einsum(
            'bhsk,bhsv->bhkv', k_ * jnp.exp(b_last[:, :, None, :] - b), v_)
        return S, o_inter + o_intra

    S0 = jnp.zeros((B, H, DK, DV), jnp.float32)
    _, o = lax.scan(step, S0, (qc, kc, vc, gc))
    return o.transpose(1, 0, 3, 2, 4).reshape(B, T, H, DV)

def _hgrn2_mixer(h, w_in, w_out, g_norm, lb):
    B, T, _ = h.shape
    proj = h @ w_in
    zq, zf, zi, zg = jnp.split(proj, [HG_F_DIM, 2 * HG_F_DIM, 2 * HG_F_DIM + HG_V_DIM], axis=-1)
    zf = zf.astype(jnp.float32)
    lb = lb.astype(jnp.float32)
    log_f = jnp.logaddexp(jnp.log(lb), jnp.log1p(-lb) + jax.nn.log_sigmoid(zf))
    k = (1.0 - lb) * jax.nn.sigmoid(-zf)
    q = jax.nn.silu(zq.astype(jnp.float32))
    heads = lambda a: a.reshape(B, T, HG_HEADS, -1)
    o = _hgrn2_chunk_scan(heads(q), heads(k), heads(zi.astype(jnp.float32)), heads(log_f))
    o = o * lax.rsqrt(jnp.mean(o * o, axis=-1, keepdims=True) + EPS) * g_norm.astype(jnp.float32)
    o = o * jax.nn.silu(heads(zg.astype(jnp.float32)))
    return o.reshape(B, T, HG_V_DIM).astype(h.dtype) @ w_out

def _band(a, nc):
    pad = jnp.pad(a, ((0, 0), (WINDOW_CHUNKS - 1, 0), (0, 0), (0, 0), (0, 0)))
    return jnp.concatenate([pad[:, j:j + nc] for j in range(WINDOW_CHUNKS)], axis=2)

def _shared_kv(x, c_act, kv_ada_w, kv_ada_b, kv_norm, kv_w, kv_b):
    B, T, _ = x.shape
    nc = T // CHUNK
    shift, scale = jnp.split(c_act @ kv_ada_w + kv_ada_b, 2, axis=-1)
    h = _modulate(_rmsnorm(x, kv_norm), shift, scale)
    k, v = jnp.split(h @ kv_w + kv_b, 2, axis=-1)
    shp = (B, nc, CHUNK, SW_KV_HEADS, SW_HEAD_DIM)
    return _band(k.reshape(shp), nc), _band(v.reshape(shp), nc)

def _swa_sink_mixer(h, k_band, v_band, w_q, b_q, w_o, sinks):
    B, T, _ = h.shape
    nc = T // CHUNK
    q = (h @ w_q + b_q).reshape(B, nc, CHUNK, SW_KV_HEADS, SW_GROUP, SW_HEAD_DIM)
    s = jnp.einsum('bnqhgd,bnkhd->bhgnqk', q, k_band).astype(jnp.float32) * (SW_HEAD_DIM ** -0.5)
    key_chunk = jnp.arange(nc)[:, None] - (WINDOW_CHUNKS - 1) + jnp.arange(WINDOW_CHUNKS)[None, :]
    valid = jnp.repeat(key_chunk >= 0, CHUNK, axis=1)
    s = jnp.where(valid[:, None, :], s, -jnp.inf)
    sink = jnp.broadcast_to(
        sinks.astype(jnp.float32).reshape(1, SW_KV_HEADS, SW_GROUP, 1, 1, 1), s.shape[:-1] + (1,))
    p = jax.nn.softmax(jnp.concatenate([s, sink], axis=-1), axis=-1)[..., :-1]
    o = jnp.einsum('bhgnqk,bnkhd->bnqhgd', p.astype(v_band.dtype), v_band).reshape(B, T, D_MODEL)
    return o @ w_o

def setup_inputs(seed: int = 0) -> dict:
    key = jax.random.key(seed)
    ks = jax.random.split(key, 24)
    n = lambda k, shape, s: jax.random.normal(k, shape, jnp.float32) * s
    D = D_MODEL
    return {
        "x": n(ks[0], (BATCH, SEQ, D), 1.0),
        "c": n(ks[1], (BATCH, D), 1.0),
        "ada_w": n(ks[2], (DEPTH, D, 6 * D), 0.5 * D ** -0.5),
        "ada_b": n(ks[3], (DEPTH, 6 * D), 0.02),
        "norm_mix": 1.0 + n(ks[4], (DEPTH, D), 0.02),
        "norm_mlp": 1.0 + n(ks[5], (DEPTH, D), 0.02),
        "mlp_w1": n(ks[6], (DEPTH, D, D_FF), D ** -0.5),
        "mlp_w2": n(ks[7], (DEPTH, D_FF, D), D_FF ** -0.5),
        "hg_w_in": n(ks[8], (N_A_LAYERS, D, HG_IN_DIM), D ** -0.5),
        "hg_w_out": n(ks[9], (N_A_LAYERS, HG_V_DIM, D), HG_V_DIM ** -0.5),
        "hg_g_norm": 1.0 + n(ks[10], (N_A_LAYERS, HG_HEAD_V), 0.02),
        "hg_lb_gamma": n(ks[11], (N_A_LAYERS, HG_F_DIM), 1.0),
        "kv_ada_w": n(ks[12], (D, 2 * D), 0.5 * D ** -0.5),
        "kv_ada_b": n(ks[13], (2 * D,), 0.02),
        "kv_norm": 1.0 + n(ks[14], (D,), 0.02),
        "kv_w": n(ks[15], (D, 2 * SW_KV_DIM), D ** -0.5),
        "kv_b": n(ks[16], (2 * SW_KV_DIM,), 0.02),
        "sw_w_q": n(ks[17], (N_B_LAYERS, D, SW_Q_HEADS * SW_HEAD_DIM), D ** -0.5),
        "sw_b_q": n(ks[18], (N_B_LAYERS, SW_Q_HEADS * SW_HEAD_DIM), 0.02),
        "sw_w_o": n(ks[19], (N_B_LAYERS, SW_Q_HEADS * SW_HEAD_DIM, D), (SW_Q_HEADS * SW_HEAD_DIM) ** -0.5),
        "sw_sinks": n(ks[20], (N_B_LAYERS, SW_Q_HEADS), 1.0),
        "final_norm": 1.0 + n(ks[21], (D,), 0.02),
    }

def reference(x, c, ada_w, ada_b, norm_mix, norm_mlp, mlp_w1, mlp_w2, hg_w_in, hg_w_out,
              hg_g_norm, hg_lb_gamma, kv_ada_w, kv_ada_b, kv_norm, kv_w, kv_b,
              sw_w_q, sw_b_q, sw_w_o, sw_sinks, final_norm):
    c_act = jax.nn.silu(c)
    lb_cum = jnp.cumsum(jax.nn.softmax(hg_lb_gamma.astype(jnp.float32), axis=0), axis=0)
    lbs = jnp.maximum(lb_cum - lb_cum[0:1], 0.0)
    k_band = v_band = None
    for l in range(DEPTH):
        sh1, sc1, g1, sh2, sc2, g2 = jnp.split(c_act @ ada_w[l] + ada_b[l], 6, axis=-1)
        h = _modulate(_rmsnorm(x, norm_mix[l]), sh1, sc1)
        if l < N_A_LAYERS:
            y = _hgrn2_mixer(h, hg_w_in[l], hg_w_out[l], hg_g_norm[l], lbs[l])
        else:
            b = l - N_A_LAYERS
            y = _swa_sink_mixer(h, k_band, v_band, sw_w_q[b], sw_b_q[b], sw_w_o[b], sw_sinks[b])
        x = x + g1[:, None, :] * y
        h = _modulate(_rmsnorm(x, norm_mlp[l]), sh2, sc2)
        x = x + g2[:, None, :] * (jnp.square(jax.nn.relu(h @ mlp_w1[l])) @ mlp_w2[l])
        if l == N_A_LAYERS - 1:
            k_band, v_band = _shared_kv(x, c_act, kv_ada_w, kv_ada_b, kv_norm, kv_w, kv_b)
    return _rmsnorm(x, final_norm)


_drawn_inputs = setup_inputs


def setup_inputs(seed=0):
    import zlib

    import numpy as np

    out = dict(_drawn_inputs(seed))
    spreads = {}
    factors = {'norm_mix': 8.0,
     'norm_mlp': 4.596,
     'hg_g_norm': 8.0,
     'kv_ada_b': 8.0,
     'kv_norm': 8.0,
     'kv_b': 64.0,
     'sw_b_q': 22.281,
     'sw_sinks': 8.0,
     'final_norm': 7.791}
    for name, (base, spread) in spreads.items():
        noise = np.random.default_rng([zlib.crc32(name.encode()), seed]).standard_normal(out[name].shape)
        drawn = base * np.exp(spread * noise) if base else spread * noise
        out[name] = __import__('jax').numpy.asarray(drawn.astype(out[name].dtype))
    for name, factor in factors.items():
        out[name] = (out[name] * factor).astype(out[name].dtype)
    return out
```

```python
import concourse.bass as bass
from concourse import mybir
from contextlib import ExitStack

P = 128
T = 1024
D = 1024
KT = D // P
HALF = 512
NHALF = T // HALF
HEADS = 8
NCH = T // P
LEVELS = 7
DEPTH = 2
D_FF = 4096
GROUP = 2
NGROUPS = D_FF // P // GROUP
KV_TILES = 2
QCH = 64
EPS = 1e-6
UNIT = 1024
ADA_N = 256
ADA_KH = 4
ADA_CHUNKS = (6 * D * DEPTH + 2 * D) // ADA_N
ADA_FIRST = 2 * D // ADA_N
SCORE_SCALE = 64 ** -0.5

U_HGRN = HEADS * 4 + HEADS
U_MLP = 2 * D_FF // P
U_ATT = 4 + 8 + 8
N_UNITS = U_HGRN + DEPTH * U_MLP + U_ATT

COLS = {}
_at = 0
for _name, _n in (("c", 8), ("mix0", 8), ("mix1", 8), ("mlp0", 8), ("mlp1", 8), ("kvn", 8),
                  ("fin", 8), ("gnorm", 1), ("gamma", 8), ("kvb", 4), ("bq", 8), ("sink", 16),
                  ("adab", 112)):
    COLS[_name] = _at
    _at += _n
N_COLS = _at
SH1, SC1, G1, SH2, SC2, G2, KSH, KSC, SH1B, SC1B, G1B, SH2B, SC2B, G2B = (8 * i for i in range(14))

HG_PAIR = dict(unit=10, tile=16, set0=8, set1=8, aux=10, head=2, ada=8, red=2, rs=2)
MLP_TWO = dict(unit=8, tile=20, set0=10, set1=10, hid=4)
MLP_TWO_ADA = dict(MLP_TWO, aux=2, ada=8, red=2)


def ada_count(n):
    return n("ada", ADA_FIRST * KT, ADA_KH)


class Counts:

    def __init__(self):
        self.n = dict.fromkeys(("unit", "tile", "set0", "set1", "aux", "head", "ada", "red",
                                "rs", "hid", "sqadd", "xn", "h", "norm"), 0)
        self.i, self.per, self.start = None, {}, None

    def __call__(self, name, plus=0, times=1, over=1):
        v = self.n[name] // over * times + plus
        per = self.per.get(name, 0)
        return v + self.i * (per // over * times) if per else v

    def add(self, name, k=1):
        self.n[name] += k

    def enter(self, i, per):
        self.i, self.per, self.start = i, per, dict(self.n)

    def leave(self, times):
        for k, v in self.n.items():
            if v != self.start[k]:
                assert v - self.start[k] == self.per[k], (k, v - self.start[k])
                self.n[k] = self.start[k] + times * self.per[k]
        self.i, self.per = None, {}


def build(nc, xT, weights, ada, cols, ident_in, masks_in, outT):
    f32, f32r, u8 = mybir.dt.float32, mybir.dt.float32r, mybir.dt.uint8
    ALU, ACT, AX = mybir.AluOpType, mybir.ActivationFunctionType, mybir.AxisListType
    ctx = ExitStack()
    with ctx:
        def sb(name, shape, dt=f32):
            return ctx.enter_context(nc.sbuf_tensor(name, shape, dt))

        def sem(name):
            return ctx.enter_context(nc.semaphore(name))

        x = sb("x", [P, KT, T])
        h_hi = sb("h_hi", [P, KT, T], f32r)
        h_lo = sb("h_lo", [P, KT, T], f32r)
        raw = sb("raw", [P, 2, UNIT])
        w_hi = sb("w_hi", [P, 2, UNIT], f32r)
        w_lo = sb("w_lo", [P, 2, UNIT], f32r)
        ada_raw = sb("ada_raw", [P, 2, ADA_KH * ADA_N])
        ada_acc = sb("ada_acc", [P, 2, 2 * ADA_N])
        ident = sb("ident", [P, P])
        ones = sb("ones", [P, P])
        masks = sb("masks", [P, LEVELS * HALF + T], u8)
        vecs = sb("vecs", [P, N_COLS])
        modv = sb("modv", [P, 14 * 8])
        cact = sb("cact", [P, 8])
        lb = sb("lb", [P, 8])
        omlb = sb("omlb", [P, 8])
        small = sb("small", [P, 16, 8])
        gain = sb("gain", [P, 5, 8])
        ms = sb("ms", [P, 2, 8])
        rstd = sb("rstd", [P, 2, 8])
        mhalf = sb("mhalf", [P, 8])
        smx = sb("smx", [P, 6, 8])

        zone = sb("zone", [P, 16 * T])
        zone_at = nc.sbuf_base - 4 * 16 * T

        def over(name, tile, shape, dt=f32):
            return nc.alloc_sbuf_tensor_at(name, shape, dt, offset=zone_at + tile * 4 * T)

        def z(tile, n=1):
            return zone[:, tile * T:(tile + n) * T]

        q_b, k_b, f_b, fp_b, vt_b, v_b, a_b, kt_b, s_b, g_b, on_b = (z(i) for i in range(11))
        osq_b = vt_b
        o_hi = over("o_hi", 11, [P, 2, T], f32r)
        o_lo = over("o_lo", 13, [P, 2, T], f32r)
        sq_b = [z(9), z(10)]
        xn_b = sq_b
        acc_b, diag_b, rb_b = z(11), z(12), z(13)
        hf_b = [acc_b, diag_b]
        pro_b = [z(2 * i, 2) for i in range(4)]
        pro_acc = z(14, 2)
        stage_b = z(8)[:, 0:LEVELS * 64 + P]
        hid_hi = over("hid_hi", 0, [P, 2, GROUP, T], f32r)
        hid_lo = over("hid_lo", 4, [P, 2, GROUP, T], f32r)
        relu_b = [z(14), z(15)]
        kT = zone[:, 0:2 * T].rearrange("p (t n) -> p t n", t=2)
        v_al = zone[:, 2 * T:4 * T].rearrange("p (j n) -> p j n", n=256)
        v_sh = zone[:, 4 * T:6 * T].rearrange("p (j n) -> p j n", n=256)
        vt2_b = [z(6), z(7)]
        p_b, pt_b = z(6), z(7)
        out_b = [z(k) for k in range(KT)]
        qT = zone[:, 8 * T:16 * T].rearrange("p (a n g q) -> p a n g q", a=2, g=4, q=QCH)

        acc = [ctx.enter_context(nc.psum_tensor(f"acc{s}", [P, T], f32)) for s in range(2)]
        lev = ctx.enter_context(nc.psum_tensor("lev", [P, T], f32))
        aux = ctx.enter_context(nc.psum_tensor("aux", [P, T], f32))

        const_in = sem("const_in")
        x_in = [sem(f"x_in{k}") for k in range(KT)]
        const_set = sem("const_set")
        masks_set = sem("masks_set")
        raw_in = [sem(f"raw_in{s}") for s in range(2)]
        hi_split = sem("hi_split")
        lo_split = sem("lo_split")
        acc_ready = sem("acc_ready")
        acc_free = [sem(f"acc_free{s}") for s in range(2)]
        aux_ready, aux_free = sem("aux_ready"), sem("aux_free")
        pro_in = [sem(f"pro_in{s}") for s in range(4)]
        ada_in = [sem(f"ada_in{s}") for s in range(2)]
        ada_step = sem("ada_step")
        mod_done = sem("mod_done")
        c_sig, c_act_done, lb_exp = sem("c_sig"), sem("c_act_done"), sem("lb_exp")
        lb_step = sem("lb_step")
        gain_done = sem("gain_done")
        sq_done, sq_added = sem("sq_done"), sem("sq_added")
        ms_step, ms_ready, rstd_ready = sem("ms_step"), sem("ms_ready"), sem("rstd_ready")
        xn_done, hf_done, hhi_done, h_ready = sem("xn_done"), sem("hf_done"), sem("hhi_done"), sem("h_ready")
        f_raw, gates_done = sem("f_raw"), sem("gates_done")
        q_sig, g_sig = sem("q_sig"), sem("g_sig")
        lev_ready, lev_copied, merged = sem("lev_ready"), sem("lev_copied"), sem("merged")
        state_done, a_zero = sem("state_done"), sem("a_zero")
        osq_done, osq_summed = sem("osq_done"), sem("osq_summed")
        ohi_done, o_split = sem("ohi_done"), sem("o_split")
        sqr_done, hidhi_done, hid_done = (sem(n) for n in ("sqr_done", "hidhi_done", "hid_done"))
        s_ready, p_exp, p_done, t_ready, pt_done, o_ready = (
            sem(n) for n in ("s_ready", "p_exp", "p_done", "t_ready", "pt_done", "o_ready"))
        sm_step, snk_exp, att_done, pmask = sem("sm_step"), sem("snk_exp"), sem("att_done"), sem("pmask")
        fin_done, out_done = sem("fin_done"), sem("out_done")

        block = ctx.enter_context(nc.Block())

        def col(name, i=0, n=1):
            return vecs[:, COLS[name] + i:COLS[name] + i + n]

        def ge(eng, s, v):
            if not isinstance(v, int) or v > 0:
                eng.wait_ge(s, v)

        def halves(buf, L):
            return buf.rearrange("p (b two l) -> p b two l", two=2, l=L)

        FP_AT = {1: None}
        at = 0
        for j in range(1, LEVELS + 1):
            FP_AT[2 ** j] = at
            at += T >> j

        def fprod(L):
            return f_b if L == 1 else fp_b[:, FP_AT[L]:FP_AT[L] + T // L]

        MLP_LOOP = (NGROUPS - 2) // 2

        @block.sync
        def _(eng):
            eng.dma_start(vecs[:, :], cols).then_inc(const_in, 16)
            eng.dma_start(ident[:, :], ident_in).then_inc(const_in, 16)
            eng.dma_start(stage_b, masks_in).then_inc(const_in, 16)
            for j in range(4):
                eng.dma_start(pro_b[j].rearrange("p (h n) -> p h n", h=2),
                              ada[2 * j:2 * j + 2].rearrange("h p n -> p h n")).then_inc(pro_in[j], 16)
                for k in (2 * j, 2 * j + 1):
                    eng.dma_start(x[:, k, :], xT[k]).then_inc(x_in[k], 16)
            for u in range(2):
                eng.dma_start(raw[:, u, :], weights[u]).then_inc(raw_in[u], 16)
            for j in range(4, ADA_FIRST):
                eng.wait_ge(ada_step, KT * (j - 3))
                eng.dma_start(pro_b[j % 4].rearrange("p (h n) -> p h n", h=2),
                              ada[2 * j:2 * j + 2].rearrange("h p n -> p h n"))\
                   .then_inc(pro_in[j % 4], 16)

            with eng.Fori(1, N_UNITS // 2) as i:
                for s in range(2):
                    eng.wait_ge(lo_split, i * 2 + (s - 1))
                    eng.dma_start(raw[:, s, :], weights[i * 2 + s]).then_inc(raw_in[s], 16)

            for k in range(KT):
                eng.wait_ge(fin_done, k + 1)
                eng.dma_start(outT[k], out_b[k]).then_inc(out_done, 16)
            eng.wait_ge(out_done, 16 * KT)

        @block.gpsimd
        def _(eng):
            eng.memset(ones[:, :], 1.0).then_inc(const_set, 1)
            eng.memset(mhalf[:, :], -0.5).then_inc(const_set, 1)
            eng.wait_ge(const_in, 48)
            for j in range(LEVELS + 1):
                w = 64 if j < LEVELS else P
                at = j * HALF
                eng.tensor_copy(masks[:, at:at + NCH * w].rearrange("p (c m) -> p c m", c=NCH),
                                stage_b[:, j * 64:j * 64 + w].rearrange("p (o m) -> p o m", o=1)
                                .broadcast_to([P, NCH, w])).then_inc(masks_set, 1)
            n = Counts()

            def root():
                s = n.n["rs"] % 2
                eng.wait_ge(ms_ready, n("rs", 1))
                eng.tensor_tensor(rstd[:, s, :], ms[:, s, :], mhalf[:, :], ALU.pow)\
                   .then_inc(rstd_ready, 1)
                n.add("rs")

            eng.wait_ge(const_set, 2)
            root()
            root()
            with eng.Fori(0, 3) as i:
                n.enter(i, dict(rs=2))
                root()
                root()
                n.leave(3)
            root()
            for _ in range(4):
                root()

        @block.scalar
        def _(eng):
            n = Counts()

            def split_hi(ahead=1):
                s = (n.n["unit"] + ahead) % 2
                eng.wait_ge(raw_in[s], n("unit", 8 * (ahead - s + 2), 8))
                ge(eng, acc_ready, n("tile"))
                eng.activation(w_hi[:, s, :], raw[:, s, :], ACT.Copy).then_inc(hi_split, 1)

            def load_ada():
                s = (n.n["ada"] + 1) % 2
                eng.wait_ge(ada_step, ada_count(n))
                eng.dma_start(ada_raw[:, s, :], ada[n("ada", 2 * ADA_FIRST + 1)]).then_inc(ada_in[s], 16)

            def take(s):
                eng.wait_ge(acc_ready, n("tile", 1))
                n.add("tile")
                n.add(f"set{s}")

            def norm(first=False):
                for k in range(KT):
                    if first:
                        eng.wait_ge(x_in[k], 16)
                    else:
                        st = (n.n["tile"] + k) % 2
                        eng.wait_ge(acc_free[st], n(f"set{st}", -((KT - 1 - k) // 2)))
                    if k >= 2:
                        eng.wait_ge(sq_added, n("sqadd", k - 1))
                    eng.activation(sq_b[k % 2], x[:, k, :], ACT.Square).then_inc(sq_done, 1)
                n.add("sqadd", KT)
                n.add("aux", 2)
                eng.wait_ge(aux_ready, n("aux"))
                eng.activation(rb_b, aux[:, :], ACT.Copy).then_inc(aux_free, 1)

            def apply(g_row, shift_at):
                eng.wait_ge(gain_done, 2 * g_row + 2)
                for k in range(KT):
                    eng.wait_ge(xn_done, n("xn", k + 1))
                    if k >= 2:
                        eng.wait_ge(h_ready, n("h", k - 1))
                    eng.activation(hf_b[k % 2], xn_b[k % 2], ACT.Identity,
                                   bias=modv[:, shift_at + k:shift_at + k + 1],
                                   scale=gain[:, g_row, k:k + 1]).then_inc(hf_done, 1)
                    eng.wait_ge(hf_done, n("xn", k + 1))
                    ge(eng, acc_ready, n("tile"))
                    eng.activation(h_hi[:, k, :], hf_b[k % 2], ACT.Copy).then_inc(hhi_done, 1)
                n.add("xn", KT)
                n.add("h", KT)

            eng.wait_ge(const_in, 48)
            eng.activation(small[:, 0, :], col("c", 0, 8), ACT.Sigmoid).then_inc(c_sig, 1)
            eng.wait_ge(lb_step, 1)
            eng.activation(small[:, 2, :], small[:, 1, :], ACT.Exp).then_inc(lb_exp, 1)
            eng.dma_start(ada_raw[:, 0, :], ada[2 * ADA_FIRST]).then_inc(ada_in[0], 16)
            split_hi(0)
            norm(True)
            n.add("aux")
            apply(0, SH1)

            def slot_f(tail):
                split_hi()
                load_ada()
                if tail:
                    n.add("aux")
                    eng.wait_ge(aux_ready, n("aux"))
                    eng.activation(kt_b, aux[:, :], ACT.Copy).then_inc(aux_free, 1)
                    n.add("aux")
                take(n.n["tile"] % 2)
                eng.activation(f_b, acc_now(), ACT.Sigmoid).then_inc(f_raw, 1)
                eng.activation(k_b, acc_now(), ACT.Sigmoid, scale=-1.0).then_inc(acc_free[set_now()], 1)
                n.add("ada")
                n.add("unit")

            def set_now():
                return (n.n["tile"] - 1) % 2

            def acc_now():
                return acc[set_now()][:, :]

            def slot_q(tail):
                split_hi()
                load_ada()
                if tail:
                    n.add("aux")
                    eng.wait_ge(aux_ready, n("aux"))
                    eng.activation(osq_b, aux[:, :], ACT.Square).then_inc(osq_done, 1)
                    n.add("aux")
                take(n.n["tile"] % 2)
                eng.activation(q_b, acc_now(), ACT.Sigmoid).then_inc(q_sig, 1)
                if tail:
                    part_hi()
                n.add("ada")
                n.add("unit")

            def part_hi():
                e = (n.n["head"] + 1) % 2
                eng.wait_ge(aux_free, n("aux"))
                eng.activation(o_hi[:, e, :], g_b, ACT.Copy).then_inc(ohi_done, 1)

            def slot_i():
                split_hi()
                load_ada()
                take(n.n["tile"] % 2)
                ge(eng, osq_summed, n("head"))
                eng.activation(vt_b, acc_now(), ACT.Copy).then_inc(acc_free[set_now()], 1)
                n.add("ada")
                n.add("unit")

            def slot_g():
                split_hi()
                load_ada()
                n.add("aux")
                eng.wait_ge(aux_ready, n("aux"))
                eng.activation(v_b, aux[:, :], ACT.Copy).then_inc(aux_free, 1)
                take(n.n["tile"] % 2)
                ge(eng, o_split, n("head"))
                eng.activation(g_b, acc_now(), ACT.Sigmoid).then_inc(g_sig, 1)
                n.add("ada")
                n.add("unit")
                n.add("head")

            def slot_m(tiles, last=False):
                if not last:
                    split_hi()
                for _ in range(tiles):
                    n.add(f"set{n.n['tile'] % 2}")
                    n.add("tile")
                n.add("unit")

            def pair(first):
                for e in range(2):
                    slot_f(not (first and e == 0))
                    slot_q(not (first and e == 0))
                    slot_i()
                    if e == 0 and not first:
                        slot_m(4)
                        slot_m(4)
                    slot_g()

            pair(True)
            with eng.Fori(0, 3) as i:
                n.enter(i, HG_PAIR)
                pair(False)
                n.leave(3)
            n.add("aux")
            eng.wait_ge(aux_ready, n("aux"))
            eng.activation(kt_b, aux[:, :], ACT.Copy).then_inc(aux_free, 1)
            n.add("aux")
            n.add("aux")
            eng.wait_ge(aux_ready, n("aux"))
            eng.activation(osq_b, aux[:, :], ACT.Square).then_inc(osq_done, 1)
            n.add("aux")
            part_hi()
            slot_m(4)
            slot_m(4)

            def slot_a(ada_too):
                split_hi()
                if ada_too:
                    load_ada_or_stop()
                take(n.n["tile"] % 2)
                j = n.n["hid"] % 2
                ge(eng, hid_done, n("hid", -1))
                st = set_now()
                eng.activation(relu_b[j], acc_now(), ACT.Relu).then_inc(acc_free[st], 1)
                eng.wait_ge(acc_free[st], n(f"set{st}"))
                eng.activation(relu_b[j], relu_b[j], ACT.Square).then_inc(sqr_done, 1)
                eng.wait_ge(sqr_done, n("hid", 1))
                eng.activation(hid_hi[:, n.n["hid"] // 2 % 2, j, :], relu_b[j], ACT.Copy)\
                   .then_inc(hidhi_done, 1)
                n.add("hid")
                n.add("unit")

            def load_ada_or_stop():
                if n.i is not None or n.n["ada"] + 1 < 2 * (ADA_CHUNKS - ADA_FIRST):
                    load_ada()
                n.add("ada")

            def slot_b(ada_too, last=False):
                if ada_too:
                    load_ada_or_stop()
                slot_m(4, last)

            def mlp(ada_too, last_unit_follows):
                def first(g):
                    slot_a(ada_too)
                    slot_a(ada_too)

                def second(g):
                    slot_b(ada_too)
                    if ada_too and g < NGROUPS - 1:
                        n.add("aux")
                    slot_b(ada_too, last=g == NGROUPS - 1 and not last_unit_follows)

                first(0)
                first(1)
                second(0)
                with eng.Fori(0, MLP_LOOP) as i:
                    n.enter(i, MLP_TWO_ADA if ada_too else MLP_TWO)
                    for g in (1, 2):
                        first(g + 1)
                        second(g)
                    n.leave(MLP_LOOP)
                second(NGROUPS - 1)
                if ada_too:
                    n.add("aux")

            norm()
            apply(1, SH2)
            mlp(True, True)

            norm()
            apply(2, KSH)
            for j in range(4):
                split_hi()
                take(n.n["tile"] % 2)
                dst = kT[:, j, :] if j < 2 else vt2_b[j - 2]
                eng.activation(dst, acc_now(), ACT.Identity, bias=col("kvb", j))\
                   .then_inc(acc_free[set_now()], 1)
                n.add("unit")
            for j in range(4):
                n.add("aux")
                eng.wait_ge(aux_ready, n("aux"))
                t, w = j // 2, j % 2
                v = (v_al, v_sh)[w]
                m = 8 - w
                eng.activation(v[:, 0:m, t * P:(t + 1) * P],
                               aux[:, 0:m * P].rearrange("p (j n) -> p j n", n=P),
                               ACT.Copy).then_inc(aux_free, 1)
            apply(3, SH1B)

            def exps(b):
                eng.wait_ge(sm_step, 7 * b + 4)
                ge(eng, t_ready, b)
                if b % 8 == 0:
                    eng.wait_ge(pmask, b // 8 + 1)
                for j in range(8):
                    w = QCH if b % 8 == 0 and j // 2 % 2 == 0 else P
                    ins = eng.activation(p_b[:, j * P:j * P + w], lev[:, j * P:j * P + w], ACT.Exp,
                                         bias=smx[:, 2, j:j + 1], scale=SCORE_SCALE)
                ins.then_inc(p_exp, 1)
                eng.activation(smx[:, 4, :], smx[:, 3, :], ACT.Exp).then_inc(snk_exp, 1)

            def turn(b):
                eng.wait_ge(t_ready, b + 1)
                eng.activation(pt_b, aux[:, :], ACT.Copy).then_inc(pt_done, 1)

            def q_out():
                take(n.n["tile"] % 2)
                j = q_at[0]
                q_at[0] += 1
                eng.activation(qT[:, j // 4, :, j % 4, :], acc_now().rearrange("p (n q) -> p n q", q=QCH),
                               ACT.Identity, bias=col("bq", j))\
                   .then_inc(acc_free[set_now()], 1)
                n.add("unit")

            q_at = [0]
            for j in range(4):
                split_hi()
                q_out()
            for j in range(4):
                split_hi()
                for b in (2 * j, 2 * j + 1):
                    exps(b)
                    turn(b)
                q_out()

            q_tiles = n.n["tile"]

            def o_hi_part(p):
                for k in range(4 * p, 4 * p + 4):
                    eng.wait_ge(att_done, 8 * p + 8)
                    eng.wait_ge(acc_ready, q_tiles)
                    eng.activation(h_hi[:, k, :].rearrange("p (n q) -> p n q", q=QCH), qT[:, p, :, k % 4, :],
                                   ACT.Copy).then_inc(hhi_done, 1)

            o_hi_part(0)
            for j in range(4):
                split_hi()
                for b in (8 + 2 * j, 9 + 2 * j):
                    exps(b)
                    turn(b)
                for _ in range(2):
                    n.add(f"set{n.n['tile'] % 2}")
                    n.add("tile")
                n.add("unit")
            o_hi_part(1)
            for j in range(4):
                slot_m(2)
            norm()
            apply(4, SH2B)
            mlp(False, False)
            norm()

        @block.tensor
        def _(eng):
            n = Counts()

            def mm6(out, wh, wl, rh, rl, start, stop):
                for w, r, a, b in ((wh, rh, start, False), (wh, rl, False, False), (wl, rh, False, stop)):
                    for c in range(NHALF):
                        ins = eng.matmul(out[:, c * HALF:(c + 1) * HALF], w,
                                         r[:, c * HALF:(c + 1) * HALF], start=a, stop=b)
                return ins

            def unit(parts_hi, parts_lo, tiles=1, ready=None, inject=None):
                s = n.n["unit"] % 2
                eng.wait_ge(lo_split, n("unit", 1))
                kn = KT // tiles
                for d in range(tiles):
                    st = n.n["tile"] % 2
                    ge(eng, acc_free[st], n(f"set{st}"))
                    for k in range(kn):
                        sub = d * kn + k
                        if inject and sub in inject:
                            inject[sub]()
                        if ready:
                            ready(d, k)
                        at = (k * tiles + d) * P
                        ins = mm6(acc[st], w_hi[:, s, at:at + P], w_lo[:, s, at:at + P],
                                  parts_hi(k), parts_lo(k), k == 0, k == kn - 1)
                    ins.then_inc(acc_ready, 1)
                    n.add("tile")
                    n.add(f"set{st}")
                n.add("unit")

            def h_hi_k(k):
                return h_hi[:, k, :]

            def h_lo_k(k):
                return h_lo[:, k, :]

            def first_of_h(d, k):
                eng.wait_ge(h_ready, n("h", k - KT + 1))

            def aux_take():
                ge(eng, aux_free, n("aux"))
                n.add("aux")

            def norm():
                eng.wait_ge(sq_added, n("sqadd", KT))
                n.add("sqadd", KT)
                aux_take()
                for c in range(NCH):
                    ins = eng.matmul(aux[:, c:c + 1], acc_b[:, c * P:(c + 1) * P], ones[:, 0:1],
                                     start=True, stop=True)
                ins.then_inc(aux_ready, 1)
                aux_take()
                for c in range(NHALF):
                    ins = eng.matmul(aux[:, c * HALF:(c + 1) * HALF], ones[:, :],
                                     diag_b[:, c * HALF:(c + 1) * HALF], start=True, stop=True)
                ins.then_inc(aux_ready, 1)

            def ada_sums(at):
                s = n.n["red"] % 2
                eng.wait_ge(ada_step, n("red", ADA_FIRST * KT + 4 * ADA_KH, 4 * ADA_KH))
                for j in range(4):
                    ins = eng.matmul(aux[:, at + j:at + j + 1], ada_acc[:, s, j * P:(j + 1) * P],
                                     ones[:, 0:1], start=True, stop=True)
                n.add("red")
                return ins

            eng.wait_ge(const_in, 48)
            eng.wait_ge(const_set, 2)
            norm()
            aux_take()
            eng.wait_ge(ada_step, ADA_FIRST * KT)
            for j in range(2 * ADA_FIRST):
                ins = eng.matmul(aux[:, j:j + 1], pro_acc[:, j * P:(j + 1) * P], ones[:, 0:1],
                                 start=True, stop=True)
            ins.then_inc(aux_ready, 1)
            n.add("h", KT)

            def scores(j):
                if j == 0:
                    eng.wait_ge(acc_free[1], n("set1"))
                    eng.wait_ge(gates_done, n("head", 2, 2))
                    ge(eng, lev_copied, n("head", 0, 8))
                    for c in range(NCH):
                        ins = eng.matmul(lev[:, c * P:(c + 1) * P], k_b[:, c * P:(c + 1) * P],
                                         q_b[:, c * P:(c + 1) * P], start=True, stop=True)
                else:
                    L = 2 ** (j - 1)
                    bank = (j - 1) % 2
                    eng.wait_ge(merged, n("head", j, 8))
                    eng.wait_ge(lev_copied, n("head", max(1, j - 1), 8))
                    for c in range(NCH):
                        right = halves(q_b[:, c * P:(c + 1) * P], L)[:, :, 1, :]
                        at = bank * HALF + c * 64
                        ins = eng.matmul(lev[:, at:at + 64].rearrange("p (b l) -> p b l", l=L),
                                         k_b[:, c * P:(c + 1) * P], right, start=True, stop=True)
                ins.then_inc(lev_ready, 1)

            def turn_8(src, m=NCH, first=0):
                aux_take()
                for c in range(m):
                    ins = eng.transpose(aux[:, c * P:(c + 1) * P],
                                        src[:, first + c * P:first + (c + 1) * P], ident[:, :])
                ins.then_inc(aux_ready, 1)

            def turn_v():
                eng.wait_ge(acc_free[0], n("set0"))
                turn_8(vt_b)

            def turn_k():
                eng.wait_ge(merged, n("head", 0, 8))
                turn_8(k_b)

            def updates():
                aux_take()
                for c in range(NCH - 1):
                    eng.matmul(aux[:, c * P:(c + 1) * P], kt_b[:, c * P:(c + 1) * P],
                               v_b[:, c * P:(c + 1) * P], start=True, stop=True)
                ada_sums(T - 4).then_inc(aux_ready, 1)

            def head_out():
                eng.wait_ge(lev_copied, n("head", 0, 8))
                aux_take()
                for c in range(NCH):
                    ins = eng.matmul(aux[:, c * P:(c + 1) * P], a_b[:, c * P:(c + 1) * P],
                                     v_b[:, c * P:(c + 1) * P], start=True, stop=c == 0)
                    if c:
                        ins = eng.matmul(aux[:, c * P:(c + 1) * P], q_b[:, c * P:(c + 1) * P],
                                         s_b[:, (c - 1) * P:c * P], start=False, stop=True)
                ins.then_inc(aux_ready, 1)

            def turn_o():
                turn_8(on_b)

            def out_pair(first_wait):
                def ready(d, k):
                    if d == 0 and k == 0:
                        eng.wait_ge(o_split, first_wait)
                for _ in range(2):
                    unit(lambda k: o_hi[:, k, :], lambda k: o_lo[:, k, :], 4, ready)

            def pair(first):
                for e in range(2):
                    tail = not (first and e == 0)
                    ready = None if tail else first_of_h
                    unit(h_hi_k, h_lo_k, 1, ready, {0: turn_k, 3: updates} if tail else None)
                    unit(h_hi_k, h_lo_k, 1, None, {1: head_out, 7: turn_o} if tail else None)
                    unit(h_hi_k, h_lo_k, 1, None, {2: lambda: scores(0), 4: lambda: scores(1),
                                                   6: lambda: scores(2)})
                    if e == 0 and not first:
                        out_pair(n("head"))
                    unit(h_hi_k, h_lo_k, 1, None,
                         {0: lambda: scores(3), 1: turn_v, 2: lambda: scores(4),
                          4: lambda: scores(5), 6: lambda: scores(6), 7: lambda: scores(7)})
                    n.add("head")
                    n.add("ada", 4)

            pair(True)
            with eng.Fori(0, 3) as i:
                n.enter(i, HG_PAIR)
                pair(False)
                n.leave(3)
            turn_k()
            updates()
            head_out()
            turn_o()
            out_pair(HEADS)

            def mlp(ada_too):
                def first(g):
                    for _ in range(GROUP):
                        unit(h_hi_k, h_lo_k, 1, first_of_h if g == 0 else None)
                        n.add("hid")
                        if ada_too:
                            n.add("ada")

                def second(par, behind, sums):
                    for un in range(2):
                        def ready(d, k):
                            if un == 0 and d == 0:
                                eng.wait_ge(hid_done, n("hid", k + 1 - GROUP - behind))
                        unit(lambda k: hid_hi[:, par, k, :], lambda k: hid_lo[:, par, k, :], 4, ready,
                             {2: sums} if sums and un == 0 else None)
                        if ada_too:
                            n.add("ada")

                def sums():
                    aux_take()
                    ada_sums(0).then_inc(aux_ready, 1)

                s = sums if ada_too else None
                first(0)
                first(1)
                second(0, GROUP, s)
                with eng.Fori(0, MLP_LOOP) as i:
                    n.enter(i, MLP_TWO_ADA if ada_too else MLP_TWO)
                    for g in (1, 2):
                        first(g + 1)
                        second(g % 2, GROUP, s)
                    n.leave(MLP_LOOP)
                second((NGROUPS - 1) % 2, 0, None)
                if ada_too:
                    sums()

            norm()
            n.add("h", KT)
            mlp(True)

            norm()
            n.add("h", KT)
            for j in range(4):
                unit(h_hi_k, h_lo_k, 1, first_of_h if j == 0 else None)
            for j in range(4):
                t, w = j // 2, j % 2
                st = (n.n["tile"] + t) % 2
                eng.wait_ge(acc_free[st], n(f"set{st}"))
                turn_8(vt2_b[t], 8 - w, w * QCH)
            n.add("h", KT)
            for j in range(4):
                unit(h_hi_k, h_lo_k, 1, first_of_h if j == 0 else None)
            q_sets = [[n.n["set0"] + 2 * p, n.n["set1"] + 2 * p] for p in range(2)]
            v_turned = n("aux")

            def att_scores(b):
                p, m = b // 8, b % 8
                if m == 0:
                    for st in range(2):
                        eng.wait_ge(acc_free[st], q_sets[p][st])
                if b:
                    eng.wait_ge(p_exp, b)
                for a in range(2):
                    for c in range(2):
                        n0 = 2 * m + c
                        key = QCH * max(n0 - 1, 0)
                        for gp in range(2):
                            at = a * HALF + c * 256 + gp * P
                            ins = eng.matmul(lev[:, at:at + P],
                                             qT[64 * a:64 * a + 64, p, n0, 2 * gp:2 * gp + 2, :]
                                             .rearrange("p g q -> p (g q)"),
                                             kT[64 * a:64 * a + 64, p, key:key + P],
                                             start=True, stop=True)
                ins.then_inc(s_ready, 1)

            def att_turn(b):
                eng.wait_ge(p_done, b + 1)
                if b == 0:
                    eng.wait_ge(aux_free, v_turned)
                else:
                    eng.wait_ge(att_done, b)
                for j in range(8):
                    ins = eng.transpose(aux[:, j * P:(j + 1) * P], p_b[:, j * P:(j + 1) * P], ident[:, :])
                ins.then_inc(t_ready, 1)

            def att_out(b):
                p, m = b // 8, b % 8
                eng.wait_ge(pt_done, b + 1)
                for a in range(2):
                    for c in range(2):
                        v = v_al[:, m, :] if c or not m else v_sh[:, m - 1, :]
                        hd = (2 * p + a) * 64
                        ins = eng.matmul(aux[64 * a:64 * a + 64, c * 256:(c + 1) * 256],
                                         v[:, hd:hd + 64],
                                         pt_b[:, a * HALF + c * 256:a * HALF + (c + 1) * 256],
                                         start=True, stop=True)
                ins.then_inc(o_ready, 1)

            def two_batches(b):
                def nxt(b):
                    if b + 1 not in (8, 16):
                        att_scores(b + 1)
                return {0: (lambda: att_scores(b)) if b % 8 == 0 else (lambda: None),
                        2: lambda: att_turn(b), 3: lambda: (att_out(b), nxt(b)),
                        6: lambda: att_turn(b + 1), 7: lambda: (att_out(b + 1), nxt(b + 1))}

            for j in range(4):
                unit(h_hi_k, h_lo_k, 1, None, two_batches(2 * j))

            def o_ready_k(p):
                def ready(d, k):
                    if d == 0:
                        eng.wait_ge(h_ready, n("h", 4 * p + k + 1))
                return ready

            for p in range(2):
                for j in range(4):
                    unit(lambda k: h_hi[:, 4 * p + k, :], lambda k: h_lo[:, 4 * p + k, :], 2,
                         o_ready_k(p), two_batches(8 + 2 * j) if p == 0 else None)
            n.add("h", KT)

            norm()
            n.add("h", KT)
            mlp(False)
            norm()

        @block.vector
        def _(eng):
            n = Counts()

            def split_lo(ahead=1):
                s = (n.n["unit"] + ahead) % 2
                eng.wait_ge(hi_split, n("unit", ahead + 1))
                eng.tensor_tensor(w_lo[:, s, :], raw[:, s, :], w_hi[:, s, :].bitcast(f32), ALU.subtract)\
                   .then_inc(lo_split, 1)

            def take():
                eng.wait_ge(acc_ready, n("tile", 1))
                s = n.n["tile"] % 2
                n.add("tile")
                n.add(f"set{s}")
                return s

            def ada_unit():
                i = n.n["ada"] % 4
                s, g = n.n["ada"] % 2, n.n["ada"] // 4 % 2
                eng.wait_ge(ada_in[s], n("ada", 8 * (2 - s), 8))
                dst = ada_acc[:, g, (i // 2) * ADA_N:(i // 2 + 1) * ADA_N]
                for k in range(ADA_KH):
                    kk = (i % 2) * ADA_KH + k
                    src = ada_raw[:, s, k * ADA_N:(k + 1) * ADA_N]
                    cv = cact[:, kk:kk + 1]
                    if kk == 0:
                        ins = eng.tensor_scalar(dst, src, cv, None, ALU.mult)
                    else:
                        eng.wait_ge(ada_step, ada_steps(k))
                        ins = eng.scalar_tensor_tensor(out=dst, in0=src, scalar=cv, in1=dst,
                                                       op0=ALU.mult, op1=ALU.add)
                    ins.then_inc(ada_step, 1)
                n.add("ada")

            def ada_steps(k):
                return n("ada", ADA_FIRST * KT + k, ADA_KH)

            def mod_cols(at):
                ins = eng.tensor_tensor(modv[:, bass.ds(n("red", 16, 4), 4)], aux[:, at:at + 4],
                                        vecs[:, bass.ds(n("red", 16 + COLS["adab"], 4), 4)], ALU.add)
                n.add("red")
                return ins

            def stream(gate_at, d):
                s = take()
                eng.scalar_tensor_tensor(out=x[:, d, :], in0=acc[s][:, :],
                                         scalar=modv[:, gate_at + d:gate_at + d + 1], in1=x[:, d, :],
                                         op0=ALU.mult, op1=ALU.add)\
                   .then_inc(acc_free[s], 1)

            def norm():
                for k in range(1, KT):
                    eng.wait_ge(sq_done, n("sqadd", k + 1))
                    if k == 1:
                        eng.tensor_tensor(acc_b, sq_b[0], sq_b[1], ALU.add)\
                           .then_inc(sq_added, 2)
                    else:
                        eng.wait_ge(sq_added, n("sqadd", k))
                        eng.tensor_tensor(acc_b, acc_b, sq_b[k % 2], ALU.add).then_inc(sq_added, 1)
                n.add("sqadd", KT)
                n.add("aux")
                s = n.n["rs"] % 2
                eng.wait_ge(aux_ready, n("aux"))
                eng.tensor_scalar(ms[:, s, :], aux[:, 0:8], 1.0 / D, EPS, ALU.mult, ALU.add)\
                   .then_inc(ms_ready, 1)
                eng.wait_ge(rstd_ready, n("rs", 1))
                n.add("rs")
                eng.tensor_tensor(diag_b.rearrange("p (c t) -> p c t", t=P),
                                  ident[:, :].rearrange("p (o t) -> p o t", o=1).broadcast_to([P, NCH, P]),
                                  rstd[:, s, :].rearrange("p (c o) -> p c o", o=1).broadcast_to([P, NCH, P]),
                                  ALU.mult).then_inc(aux_free, 1)
                n.add("aux")

            def rb_ready():
                eng.wait_ge(aux_free, n("aux"))

            def gains(row, name, scale_at):
                eng.tensor_scalar(small[:, 4 + row, :], modv[:, scale_at:scale_at + 8], 1.0, None, ALU.add)\
                   .then_inc(gain_done, 1)
                eng.wait_ge(gain_done, 2 * row + 1)
                eng.tensor_tensor(gain[:, row, :], small[:, 4 + row, :], col(name, 0, 8), ALU.mult)\
                   .then_inc(gain_done, 1)

            def apply():
                for k in range(KT + 1):
                    if k < KT:
                        if k >= 2:
                            eng.wait_ge(hf_done, n("xn", k - 1))
                        eng.tensor_tensor(xn_b[k % 2], x[:, k, :], rb_b, ALU.mult).then_inc(xn_done, 1)
                    if k:
                        j = k - 1
                        eng.wait_ge(hhi_done, n("h", j + 1))
                        eng.tensor_tensor(h_lo[:, j, :], hf_b[j % 2], h_hi[:, j, :].bitcast(f32),
                                          ALU.subtract).then_inc(h_ready, 1)
                n.add("h", KT)
                n.add("xn", KT)

            eng.wait_ge(const_in, 48)
            eng.wait_ge(c_sig, 1)
            eng.tensor_tensor(cact[:, :], col("c", 0, 8), small[:, 0, :], ALU.mult).then_inc(c_act_done, 1)
            eng.tensor_tensor(small[:, 1, :], col("gamma", 0, 8), col("gamma", 0, 8), ALU.subtract)\
               .then_inc(lb_step, 1)
            eng.wait_ge(lb_exp, 1)
            eng.reciprocal(small[:, 3, :], small[:, 2, :]).then_inc(lb_step, 1)
            eng.wait_ge(lb_step, 2)
            eng.tensor_tensor(small[:, 3, :], small[:, 3, :], small[:, 2, :], ALU.mult).then_inc(lb_step, 1)
            eng.wait_ge(lb_step, 3)
            eng.tensor_tensor(lb[:, :], small[:, 3, :], small[:, 3, :], ALU.subtract).then_inc(lb_step, 1)
            eng.wait_ge(lb_step, 4)
            eng.tensor_scalar(lb[:, :], lb[:, :], 0.0, None, ALU.max).then_inc(lb_step, 1)
            eng.wait_ge(lb_step, 5)
            eng.tensor_scalar(omlb[:, :], lb[:, :], -1.0, 1.0, ALU.mult, ALU.add).then_inc(lb_step, 1)
            split_lo(0)
            eng.wait_ge(c_act_done, 1)
            for j in range(ADA_FIRST):
                eng.wait_ge(pro_in[j % 4], 16 * (j // 4 + 1))
                dst = pro_acc[:, j * ADA_N:(j + 1) * ADA_N]
                for k in range(KT):
                    src = pro_b[j % 4][:, k * ADA_N:(k + 1) * ADA_N]
                    if k == 0:
                        ins = eng.tensor_scalar(dst, src, cact[:, 0:1], None, ALU.mult)
                    else:
                        eng.wait_ge(ada_step, j * KT + k)
                        ins = eng.scalar_tensor_tensor(out=dst, in0=src, scalar=cact[:, k:k + 1],
                                                       in1=dst, op0=ALU.mult, op1=ALU.add)
                    ins.then_inc(ada_step, 1)
            norm()
            rb_ready()
            n.add("aux")
            eng.wait_ge(aux_ready, n("aux"))
            eng.tensor_tensor(modv[:, 0:16], aux[:, 0:16], col("adab", 0, 16), ALU.add)\
               .then_inc(aux_free, 1)
            eng.wait_ge(aux_free, n("aux"))
            gains(0, "mix0", SC1)
            apply()
            eng.memset(a_b, 0.0).then_inc(a_zero, 1)
            eng.wait_ge(masks_set, LEVELS + 1)

            def merge(j):
                if j == 1:
                    eng.wait_ge(lev_ready, n("head", 1, 8))
                    eng.tensor_tensor(q_b, q_b, f_b, ALU.mult).then_inc(merged, 1)
                    return
                L = 2 ** (j - 2)
                eng.wait_ge(lev_ready, n("head", j, 8))
                eng.wait_ge(merged, n("head", j - 1, 8))
                eng.wait_ge(lev_copied, n("head", j - 1, 8))
                fl = fprod(L).rearrange("p (b two) -> p b two", two=2)
                even, odd = fl[:, :, 0:1], fl[:, :, 1:2]
                nb = T // (2 * L)
                eng.tensor_tensor(fprod(2 * L).rearrange("p (b o) -> p b o", o=1), even, odd, ALU.mult)
                qr, kl = halves(q_b, L)[:, :, 1, :], halves(k_b, L)[:, :, 0, :]
                eng.tensor_tensor(qr, qr, even.broadcast_to([P, nb, L]), ALU.mult)
                eng.tensor_tensor(kl, kl, odd.broadcast_to([P, nb, L]), ALU.mult).then_inc(merged, 1)

            def keep(j):
                if j == 0:
                    eng.copy_predicated(a_b, masks[:, LEVELS * HALF:], lev[:, :]).then_inc(lev_copied, 1)
                    return
                L = 2 ** (j - 1)
                bank = (j - 1) % 2
                eng.copy_predicated(
                    halves(a_b, L)[:, :, 1, :],
                    masks[:, (j - 1) * HALF:j * HALF].rearrange("p (b l) -> p b l", l=L),
                    lev[:, bank * HALF:(bank + 1) * HALF].rearrange("p (b l) -> p b l", l=L))\
                   .then_inc(lev_copied, 1)

            def states():
                n.add("aux")
                eng.wait_ge(aux_ready, n("aux"))
                mod_cols(T - 4).then_inc(mod_done, 1)
                decay = fprod(P)
                eng.tensor_copy(s_b[:, 0:P], aux[:, 0:P]).then_inc(state_done, 1)
                last = NCH - 2
                for c in range(1, last + 1):
                    eng.wait_ge(state_done, n("head", c - last, last))
                    eng.scalar_tensor_tensor(out=s_b[:, c * P:(c + 1) * P],
                                                   in0=s_b[:, (c - 1) * P:c * P],
                                                   scalar=decay[:, c:c + 1],
                                                   in1=aux[:, c * P:(c + 1) * P],
                                                   op0=ALU.mult, op1=ALU.add)\
                       .then_inc(aux_free if c == last else state_done, 1)

            def norm_out():
                n.add("aux")
                s = n.n["rs"] % 2
                eng.wait_ge(osq_done, n("head"))
                eng.tensor_reduce(small[:, 15, :], osq_b.rearrange("p (c v) -> p c v", v=P), AX.X, ALU.add)\
                   .then_inc(osq_summed, 1)
                eng.wait_ge(osq_summed, n("head"))
                eng.tensor_scalar(ms[:, s, :], small[:, 15, :], 1.0 / P, EPS, ALU.mult, ALU.add)\
                   .then_inc(ms_ready, 1)
                eng.wait_ge(rstd_ready, n("rs", 1))
                n.add("rs")
                eng.tensor_tensor(on_b.rearrange("p (c v) -> p c v", v=P),
                                  aux[:, :].rearrange("p (c v) -> p c v", v=P),
                                  rstd[:, s, :].rearrange("p (c o) -> p c o", o=1).broadcast_to([P, NCH, P]),
                                  ALU.mult).then_inc(aux_free, 1)

            def gate_out():
                n.add("aux")
                eng.wait_ge(acc_free[1], n("set1"))
                eng.wait_ge(aux_ready, n("aux"))
                eng.scalar_tensor_tensor(out=g_b, in0=aux[:, :], scalar=col("gnorm"), in1=g_b,
                                         op0=ALU.mult, op1=ALU.mult)\
                   .then_inc(aux_free, 1)

            def part_lo():
                e = (n.n["head"] + 1) % 2
                eng.wait_ge(ohi_done, n("head"))
                eng.tensor_tensor(o_lo[:, e, :], g_b, o_hi[:, e, :].bitcast(f32), ALU.subtract)\
                   .then_inc(o_split, 1)

            def slot_f(tail):
                split_lo()
                ada_unit()
                if tail:
                    n.add("aux")
                    states()
                s = take()
                hd = n("head")
                eng.wait_ge(f_raw, n("head", 1))
                eng.tensor_scalar(f_b, f_b, omlb[:, bass.ds(hd, 1)], lb[:, bass.ds(hd, 1)],
                                  ALU.mult, ALU.add).then_inc(gates_done, 1)
                eng.wait_ge(acc_free[s], n(f"set{s}"))
                eng.tensor_scalar(k_b, k_b, omlb[:, bass.ds(hd, 1)], None, ALU.mult)\
                   .then_inc(gates_done, 1)
                n.add("unit")

            def slot_q(tail):
                split_lo()
                ada_unit()
                if tail:
                    norm_out()
                    gate_out()
                s = take()
                eng.wait_ge(q_sig, n("head", 1))
                eng.tensor_tensor(q_b, q_b, acc[s][:, :], ALU.mult)\
                   .then_inc(acc_free[s], 1)
                if tail:
                    part_lo()
                n.add("unit")

            def slot_i(first_a):
                split_lo()
                ada_unit()
                if first_a:
                    eng.wait_ge(a_zero, 1)
                eng.wait_ge(gates_done, n("head", 2, 2))
                eng.wait_ge(acc_free[1], n("set1"))
                for j in range(3):
                    merge(j + 1)
                    keep(j)
                take()
                n.add("unit")

            def slot_g():
                split_lo()
                ada_unit()
                n.add("aux")
                for j in range(3, 8):
                    merge(j + 1)
                    keep(j)
                s = take()
                eng.wait_ge(g_sig, n("head", 1))
                eng.tensor_tensor(g_b, g_b, acc[s][:, :], ALU.mult)\
                   .then_inc(acc_free[s], 1)
                n.add("unit")
                n.add("head")

            def pair(first):
                for e in range(2):
                    tail = not (first and e == 0)
                    slot_f(tail)
                    slot_q(tail)
                    slot_i(first and e == 0)
                    if e == 0 and not first:
                        for un in range(2):
                            split_lo()
                            for d in range(4):
                                stream(G1, 4 * un + d)
                            n.add("unit")
                    slot_g()

            pair(True)
            with eng.Fori(0, 3) as i:
                n.enter(i, HG_PAIR)
                pair(False)
                n.leave(3)
            n.add("aux")
            states()
            norm_out()
            gate_out()
            part_lo()
            for un in range(2):
                split_lo()
                for d in range(4):
                    stream(G1, 4 * un + d)
                n.add("unit")

            def mlp(ada_too, gate_at, unit_follows):
                def first(g):
                    for _ in range(GROUP):
                        split_lo()
                        if ada_too:
                            ada_unit()
                        take()
                        j = n.n["hid"] % 2
                        eng.wait_ge(hidhi_done, n("hid", 1))
                        par = n.n["hid"] // 2 % 2
                        eng.tensor_tensor(hid_lo[:, par, j, :], relu_b[j],
                                          hid_hi[:, par, j, :].bitcast(f32), ALU.subtract)\
                           .then_inc(hid_done, 1)
                        n.add("hid")
                        n.add("unit")

                def second(g, sums):
                    for un in range(2):
                        if g < NGROUPS - 1 or un == 0 or unit_follows:
                            split_lo()
                        if ada_too:
                            ada_unit()
                        for d in range(4):
                            stream(gate_at, 4 * un + d)
                            if sums and un == 0 and d == 0:
                                group_cols()
                        n.add("unit")

                def group_cols():
                    n.add("aux")
                    eng.wait_ge(aux_ready, n("aux"))
                    mod_cols(0).then_inc(aux_free, 1)

                first(0)
                first(1)
                second(0, ada_too)
                with eng.Fori(0, MLP_LOOP) as i:
                    n.enter(i, MLP_TWO_ADA if ada_too else MLP_TWO)
                    for g in (1, 2):
                        first(g + 1)
                        second(g, ada_too)
                    n.leave(MLP_LOOP)
                second(NGROUPS - 1, False)
                if ada_too:
                    group_cols()

            eng.wait_ge(mod_done, HEADS)
            gains(1, "mlp0", SC2)
            norm()
            rb_ready()
            apply()
            mlp(True, G2, True)

            eng.wait_ge(aux_free, n("aux"))
            gains(2, "kvn", KSC)
            gains(3, "mix1", SC1B)
            norm()
            rb_ready()
            apply()
            for j in range(4):
                split_lo()
                take()
                n.add("unit")
            n.add("aux", 4)
            apply()

            def blocks(buf):
                return buf.rearrange("p (j n) -> p j n", n=P)

            def maxima(b):
                eng.wait_ge(s_ready, b + 1)
                if b % 8 == 0:
                    for a in range(2):
                        for c in range(2):
                            j = 4 * a + 2 * c
                            w = P if c else QCH
                            ins = eng.tensor_reduce(smx[:, 0, j:j + 2],
                                                    blocks(lev[:, :])[:, j:j + 2, 0:w], AX.X, ALU.max)
                    ge(eng, t_ready, b)
                    for a in range(2):
                        zero = eng.memset(blocks(p_b)[:, 4 * a:4 * a + 2, QCH:P], 0.0)
                    zero.then_inc(pmask, 1)
                else:
                    ins = eng.tensor_reduce(smx[:, 0, :], blocks(lev[:, :]), AX.X, ALU.max)
                ins.then_inc(sm_step, 1)
                sink = col("sink", 8 * (b // 8), 8)
                eng.wait_ge(sm_step, 7 * b + 1)
                eng.scalar_tensor_tensor(out=smx[:, 1, :], in0=smx[:, 0, :], scalar=SCORE_SCALE,
                                         in1=sink, op0=ALU.mult, op1=ALU.max).then_inc(sm_step, 1)
                eng.wait_ge(sm_step, 7 * b + 2)
                eng.tensor_scalar(smx[:, 2, :], smx[:, 1, :], -1.0, None, ALU.mult).then_inc(sm_step, 1)
                eng.tensor_tensor(smx[:, 3, :], sink, smx[:, 1, :], ALU.subtract).then_inc(sm_step, 1)

            def normalise(b):
                eng.wait_ge(p_exp, b + 1)
                eng.tensor_reduce(smx[:, 5, :], blocks(p_b), AX.X, ALU.add).then_inc(sm_step, 1)
                eng.wait_ge(snk_exp, b + 1)
                eng.wait_ge(sm_step, 7 * b + 5)
                eng.tensor_tensor(smx[:, 5, :], smx[:, 5, :], smx[:, 4, :], ALU.add).then_inc(sm_step, 1)
                eng.wait_ge(sm_step, 7 * b + 6)
                eng.reciprocal(smx[:, 1, :], smx[:, 5, :]).then_inc(sm_step, 1)
                eng.wait_ge(sm_step, 7 * b + 7)
                eng.tensor_tensor(blocks(p_b), blocks(p_b),
                                  smx[:, 1, :].rearrange("p (j o) -> p j o", o=1).broadcast_to([P, 8, P]),
                                  ALU.mult).then_inc(p_done, 1)

            def heads_out(b):
                p, m = b // 8, b % 8
                eng.wait_ge(o_ready, b + 1)
                eng.tensor_copy(qT[:, p, 2 * m:2 * m + 2, :, :].rearrange("p c g q -> p (c g q)"),
                                aux[:, 0:HALF]).then_inc(att_done, 1)

            def batch(b):
                maxima(b)
                normalise(b)
                heads_out(b)

            def o_lo_part(p):
                for k in range(4 * p, 4 * p + 4):
                    eng.wait_ge(hhi_done, n("h", k + 1))
                    eng.tensor_tensor(h_lo[:, k, :].rearrange("p (n q) -> p n q", q=QCH),
                                      qT[:, p, :, k % 4, :],
                                      h_hi[:, k, :].bitcast(f32).rearrange("p (n q) -> p n q", q=QCH),
                                      ALU.subtract).then_inc(h_ready, 1)

            for j in range(8):
                split_lo()
                if j >= 4:
                    batch(2 * j - 8)
                    batch(2 * j - 7)
                take()
                n.add("unit")
            o_lo_part(0)
            for p in range(2):
                for j in range(4):
                    split_lo()
                    for d in range(2):
                        if p == 0:
                            batch(8 + 2 * j + d)
                        stream(G1B, 2 * j + d)
                    n.add("unit")
                if p == 0:
                    o_lo_part(1)
            n.add("h", KT)

            gains(4, "mlp1", SC2B)
            norm()
            rb_ready()
            apply()
            mlp(False, G2B, False)
            norm()
            rb_ready()
            for k in range(KT):
                eng.scalar_tensor_tensor(out=out_b[k], in0=x[:, k, :], scalar=col("fin", k), in1=rb_b,
                                         op0=ALU.mult, op1=ALU.mult).then_inc(fin_done, 1)


def kernel(**inputs):
    import numpy as np
    import concourse.bacc as bacc
    from concourse.bass_utils import run_bass_kernel_spmd

    a = {k: np.asarray(v) for k, v in inputs.items()}
    f32 = mybir.dt.float32

    def square_units(w):
        k, m = w.shape
        return w.reshape(KT, P, m // P, P).transpose(2, 1, 0, 3).reshape(m // P, P, UNIT)

    def wide_units(w, kn):
        r, m = w.shape
        wide = UNIT // kn
        return w.reshape(r // (kn * P), kn, P, m // wide, wide).transpose(0, 3, 2, 1, 4)\
                .reshape(-1, P, UNIT)

    def by_pairs(w):
        return w.reshape((2, 2, 4, 64) + w.shape[1:]).transpose((0, 2, 1, 3) + tuple(range(4, 3 + w.ndim)))\
                .reshape(w.shape)

    w_in, w_out = a["hg_w_in"][0], a["hg_w_out"][0]
    uq, uf, ui, ug = (square_units(w_in[:, i * D:(i + 1) * D]) for i in range(4))
    uo = wide_units(w_out, 2)
    units = []
    for pr in range(HEADS // 2):
        for e in range(2):
            hd = 2 * pr + e
            units += [uf[hd], uq[hd], ui[hd]]
            if e == 0 and pr:
                units += [uo[2 * pr - 2], uo[2 * pr - 1]]
            units += [ug[hd]]
    units += [uo[6], uo[7]]

    def mlp_units(l):
        u1, u2 = square_units(a["mlp_w1"][l]), wide_units(a["mlp_w2"][l], GROUP)
        out = [u1[0], u1[1]]
        for g in range(NGROUPS):
            if g + 1 < NGROUPS:
                out += [u1[2 * g + 2], u1[2 * g + 3]]
            out += [u2[2 * g], u2[2 * g + 1]]
        return out

    units += mlp_units(0)
    units += list(square_units(a["kv_w"]))
    units += list(square_units(by_pairs(a["sw_w_q"][0].T).T))
    units += list(wide_units(by_pairs(a["sw_w_o"][0]), 4))
    units += mlp_units(1)
    weights = np.stack(units)
    assert weights.shape == (N_UNITS, P, UNIT)

    ada = np.concatenate([a["ada_w"][0], a["kv_ada_w"], a["ada_w"][1]], axis=1)
    ada = ada.reshape(2, ADA_KH, P, ADA_CHUNKS, ADA_N).transpose(3, 0, 2, 1, 4)\
             .reshape(2 * ADA_CHUNKS, P, ADA_KH * ADA_N)

    def columns(v):
        return v.reshape(-1, P).T

    sinks = a["sw_sinks"][0].reshape(2, 2, 2, 2)
    sink = np.empty((P, 2, 2, 2, 2), sinks.dtype)
    for g2 in range(2):
        sink[64 * g2:64 * g2 + 64] = sinks[None, :, :, None, :, g2]
    parts = dict(c=columns(a["c"][0]), mix0=columns(a["norm_mix"][0]), mix1=columns(a["norm_mix"][1]),
                 mlp0=columns(a["norm_mlp"][0]), mlp1=columns(a["norm_mlp"][1]),
                 kvn=columns(a["kv_norm"]), fin=columns(a["final_norm"]),
                 gnorm=columns(a["hg_g_norm"][0]), gamma=columns(a["hg_lb_gamma"][0]),
                 kvb=columns(a["kv_b"]), bq=columns(by_pairs(a["sw_b_q"][0])),
                 sink=sink.reshape(P, 16),
                 adab=columns(np.concatenate([a["ada_b"][0], a["kv_ada_b"], a["ada_b"][1]])))
    cols = np.ascontiguousarray(np.concatenate([parts[k] for k in COLS], axis=1))

    key, query = np.arange(P)[:, None], np.arange(P)[None, :]
    masks = []
    for j in range(LEVELS):
        L = 2 ** j
        pairs = (key // (2 * L) == query // (2 * L)) & (key // L % 2 == 0)
        masks.append(pairs[:, query[0] // L % 2 == 1])
    masks = np.concatenate(masks + [key == query], axis=1).astype(np.float32)

    arrays = {
        "xT": np.ascontiguousarray(a["x"][0].T).reshape(KT, P, T),
        "weights": weights, "ada": np.ascontiguousarray(ada), "cols": cols,
        "ident": np.eye(P, dtype=np.float32), "masks": masks,
    }
    nc = bacc.Bacc("TRN2", target_bir_lowering=False, num_devices=1)
    aps = [nc.dram_tensor("in_" + k, v.shape, mybir.dt.from_np(v.dtype), kind="ExternalInput").ap()
           for k, v in arrays.items()]
    out = nc.dram_tensor("outT", (KT, P, T), f32, kind="ExternalOutput").ap()
    build(nc, *aps, out)
    r = run_bass_kernel_spmd(nc, [{"in_" + k: v for k, v in arrays.items()}], core_ids=[0])
    return np.ascontiguousarray(r.results[0]["outT"].reshape(D, T).T)[None]
```

```python
import concourse.bass as bass
from concourse import mybir
from contextlib import ExitStack

P = 128
T = 1024
D = 1024
KT = D // P
HALF = 512
NHALF = T // HALF
HEADS = 8
NCH = T // P
LEVELS = 7
DEPTH = 2
D_FF = 4096
GROUP = 2
NGROUPS = D_FF // P // GROUP
KV_TILES = 2
QCH = 64
EPS = 1e-6
UNIT = 1024
ADA_N = 256
ADA_KH = 4
ADA_CHUNKS = (6 * D * DEPTH + 2 * D) // ADA_N
ADA_FIRST = 2 * D // ADA_N
SCORE_SCALE = 64 ** -0.5

U_HGRN = HEADS * 4 + HEADS
U_MLP = 2 * D_FF // P
U_ATT = 4 + 8 + 8
N_UNITS = U_HGRN + DEPTH * U_MLP + U_ATT

COLS = {}
_at = 0
for _name, _n in (("c", 8), ("mix0", 8), ("mix1", 8), ("mlp0", 8), ("mlp1", 8), ("kvn", 8),
                  ("fin", 8), ("gnorm", 1), ("gamma", 8), ("kvb", 4), ("bq", 8), ("sink", 16),
                  ("adab", 112)):
    COLS[_name] = _at
    _at += _n
N_COLS = _at
SH1, SC1, G1, SH2, SC2, G2, KSH, KSC, SH1B, SC1B, G1B, SH2B, SC2B, G2B = (8 * i for i in range(14))

HG_PAIR = dict(unit=10, tile=16, set0=8, set1=8, aux=10, head=2, ada=8, red=2, rs=2)
MLP_TWO = dict(unit=8, tile=20, set0=10, set1=10, hid=4)
MLP_TWO_ADA = dict(MLP_TWO, aux=2, ada=8, red=2)


def ada_count(n):
    return n("ada", ADA_FIRST * KT, ADA_KH)


class Counts:

    def __init__(self):
        self.n = dict.fromkeys(("unit", "tile", "set0", "set1", "aux", "head", "ada", "red",
                                "rs", "hid", "sqadd", "xn", "h", "norm"), 0)
        self.i, self.per, self.start = None, {}, None

    def __call__(self, name, plus=0, times=1, over=1):
        v = self.n[name] // over * times + plus
        per = self.per.get(name, 0)
        return v + self.i * (per // over * times) if per else v

    def add(self, name, k=1):
        self.n[name] += k

    def enter(self, i, per):
        self.i, self.per, self.start = i, per, dict(self.n)

    def leave(self, times):
        for k, v in self.n.items():
            if v != self.start[k]:
                assert v - self.start[k] == self.per[k], (k, v - self.start[k])
                self.n[k] = self.start[k] + times * self.per[k]
        self.i, self.per = None, {}


def build(nc, xT, weights, ada, cols, ident_in, masks_in, outT):
    f32, f32r, u8 = mybir.dt.float32, mybir.dt.float32r, mybir.dt.uint8
    ALU, ACT, AX = mybir.AluOpType, mybir.ActivationFunctionType, mybir.AxisListType
    ctx = ExitStack()
    with ctx:
        def sb(name, shape, dt=f32):
            return ctx.enter_context(nc.sbuf_tensor(name, shape, dt))

        def sem(name):
            return ctx.enter_context(nc.semaphore(name))

        x = sb("x", [P, KT, T])
        h_hi = sb("h_hi", [P, KT, T], f32r)
        h_lo = sb("h_lo", [P, KT, T], f32r)
        raw = sb("raw", [P, 2, UNIT])
        w_hi = sb("w_hi", [P, 2, UNIT], f32r)
        w_lo = sb("w_lo", [P, 2, UNIT], f32r)
        ada_raw = sb("ada_raw", [P, 2, ADA_KH * ADA_N])
        ada_acc = sb("ada_acc", [P, 2, 2 * ADA_N])
        ident = sb("ident", [P, P])
        ones = sb("ones", [P, P])
        masks = sb("masks", [P, LEVELS * HALF + T], u8)
        vecs = sb("vecs", [P, N_COLS])
        modv = sb("modv", [P, 14 * 8])
        cact = sb("cact", [P, 8])
        lb = sb("lb", [P, 8])
        omlb = sb("omlb", [P, 8])
        small = sb("small", [P, 16, 8])
        gain = sb("gain", [P, 5, 8])
        ms = sb("ms", [P, 2, 8])
        rstd = sb("rstd", [P, 2, 8])
        mhalf = sb("mhalf", [P, 8])
        smx = sb("smx", [P, 6, 8])

        zone = sb("zone", [P, 16 * T])
        zone_at = nc.sbuf_base - 4 * 16 * T

        def over(name, tile, shape, dt=f32):
            return nc.alloc_sbuf_tensor_at(name, shape, dt, offset=zone_at + tile * 4 * T)

        def z(tile, n=1):
            return zone[:, tile * T:(tile + n) * T]

        q_b, k_b, f_b, fp_b, vt_b, v_b, a_b, kt_b, s_b, g_b, on_b = (z(i) for i in range(11))
        osq_b = vt_b
        o_hi = over("o_hi", 11, [P, 2, T], f32r)
        o_lo = over("o_lo", 13, [P, 2, T], f32r)
        sq_b = [z(9), z(10)]
        xn_b = sq_b
        sum_b, rb_b, diag_b = z(8), z(13), z(12)
        hf_b = [z(11), z(12)]
        pro_b = [z(2 * i, 2) for i in range(4)]
        pro_acc = z(14, 2)
        stage_b = z(11)[:, 0:LEVELS * 64 + P]
        hid_hi = over("hid_hi", 0, [P, 2, GROUP, T], f32r)
        hid_lo = over("hid_lo", 4, [P, 2, GROUP, T], f32r)
        relu_b = [z(14), z(15)]
        kT = zone[:, 0:2 * T].rearrange("p (t n) -> p t n", t=2)
        v_al = zone[:, 2 * T:4 * T].rearrange("p (j n) -> p j n", n=256)
        v_sh = zone[:, 4 * T:6 * T].rearrange("p (j n) -> p j n", n=256)
        vt2_b = [z(6), z(7)]
        p_b, pt_b = z(6), z(7)
        out_b = [z(k) for k in range(KT)]
        qT = zone[:, 8 * T:16 * T].rearrange("p (a n g q) -> p a n g q", a=2, g=4, q=QCH)

        acc = [ctx.enter_context(nc.psum_tensor(f"acc{s}", [P, T], f32)) for s in range(2)]
        lev = ctx.enter_context(nc.psum_tensor("lev", [P, T], f32))
        aux = ctx.enter_context(nc.psum_tensor("aux", [P, T], f32))

        const_in = sem("const_in")
        x_in = [sem(f"x_in{k}") for k in range(KT)]
        const_set = sem("const_set")
        masks_set = sem("masks_set")
        raw_in = [sem(f"raw_in{s}") for s in range(2)]
        hi_split = sem("hi_split")
        lo_split = sem("lo_split")
        acc_ready = sem("acc_ready")
        acc_free = [sem(f"acc_free{s}") for s in range(2)]
        aux_ready, aux_free = sem("aux_ready"), sem("aux_free")
        pro_in = [sem(f"pro_in{s}") for s in range(4)]
        ada_in = [sem(f"ada_in{s}") for s in range(2)]
        ada_step = sem("ada_step")
        mod_done = sem("mod_done")
        c_sig, c_act_done, lb_exp = sem("c_sig"), sem("c_act_done"), sem("lb_exp")
        lb_step = sem("lb_step")
        gain_done = sem("gain_done")
        sq_done, sq_added = sem("sq_done"), sem("sq_added")
        ms_step, ms_ready, rstd_ready = sem("ms_step"), sem("ms_ready"), sem("rstd_ready")
        xn_done, hf_done, hhi_done, h_ready = sem("xn_done"), sem("hf_done"), sem("hhi_done"), sem("h_ready")
        f_raw, gates_done = sem("f_raw"), sem("gates_done")
        q_sig, g_sig = sem("q_sig"), sem("g_sig")
        lev_ready, lev_copied, merged = sem("lev_ready"), sem("lev_copied"), sem("merged")
        state_done, a_zero = sem("state_done"), sem("a_zero")
        osq_done, osq_summed = sem("osq_done"), sem("osq_summed")
        ohi_done, o_split = sem("ohi_done"), sem("o_split")
        sqr_done, hidhi_done, hid_done = (sem(n) for n in ("sqr_done", "hidhi_done", "hid_done"))
        s_ready, p_exp, p_done, t_ready, pt_done, o_ready = (
            sem(n) for n in ("s_ready", "p_exp", "p_done", "t_ready", "pt_done", "o_ready"))
        sm_step, snk_exp, att_done, pmask = sem("sm_step"), sem("snk_exp"), sem("att_done"), sem("pmask")
        fin_done, out_done = sem("fin_done"), sem("out_done")

        block = ctx.enter_context(nc.Block())

        def col(name, i=0, n=1):
            return vecs[:, COLS[name] + i:COLS[name] + i + n]

        def ge(eng, s, v):
            if not isinstance(v, int) or v > 0:
                eng.wait_ge(s, v)

        def halves(buf, L):
            return buf.rearrange("p (b two l) -> p b two l", two=2, l=L)

        FP_AT = {1: None}
        at = 0
        for j in range(1, LEVELS + 1):
            FP_AT[2 ** j] = at
            at += T >> j

        def fprod(L):
            return f_b if L == 1 else fp_b[:, FP_AT[L]:FP_AT[L] + T // L]

        MLP_LOOP = (NGROUPS - 2) // 2

        @block.sync
        def _(eng):
            eng.dma_start(vecs[:, :], cols).then_inc(const_in, 16)
            eng.dma_start(ident[:, :], ident_in).then_inc(const_in, 16)
            eng.dma_start(stage_b, masks_in).then_inc(const_in, 16)
            for k in range(KT):
                eng.dma_start(x[:, k, :], xT[k]).then_inc(x_in[k], 16)
            for j in range(4):
                eng.dma_start(pro_b[j].rearrange("p (h n) -> p h n", h=2),
                              ada[2 * j:2 * j + 2].rearrange("h p n -> p h n")).then_inc(pro_in[j], 16)
            for j in range(4, ADA_FIRST):
                eng.wait_ge(ada_step, KT * (j - 3))
                eng.dma_start(pro_b[j % 4].rearrange("p (h n) -> p h n", h=2),
                              ada[2 * j:2 * j + 2].rearrange("h p n -> p h n"))\
                   .then_inc(pro_in[j % 4], 16)
            for u in range(2):
                eng.dma_start(raw[:, u, :], weights[u]).then_inc(raw_in[u], 16)

            with eng.Fori(1, N_UNITS // 2) as i:
                for s in range(2):
                    eng.wait_ge(lo_split, i * 2 + (s - 1))
                    eng.dma_start(raw[:, s, :], weights[i * 2 + s]).then_inc(raw_in[s], 16)

            for k in range(KT):
                eng.wait_ge(fin_done, k + 1)
                eng.dma_start(outT[k], out_b[k]).then_inc(out_done, 16)
            eng.wait_ge(out_done, 16 * KT)

        @block.gpsimd
        def _(eng):
            eng.memset(ones[:, :], 1.0).then_inc(const_set, 1)
            eng.memset(mhalf[:, :], -0.5).then_inc(const_set, 1)
            eng.wait_ge(const_in, 48)
            for j in range(LEVELS + 1):
                w = 64 if j < LEVELS else P
                at = j * HALF
                eng.tensor_copy(masks[:, at:at + NCH * w].rearrange("p (c m) -> p c m", c=NCH),
                                stage_b[:, j * 64:j * 64 + w].rearrange("p (o m) -> p o m", o=1)
                                .broadcast_to([P, NCH, w])).then_inc(masks_set, 1)
            n = Counts()

            def root():
                s = n.n["rs"] % 2
                eng.wait_ge(ms_ready, n("rs", 1))
                eng.tensor_tensor(rstd[:, s, :], ms[:, s, :], mhalf[:, :], ALU.pow)\
                   .then_inc(rstd_ready, 1)
                n.add("rs")

            eng.wait_ge(const_set, 2)
            root()
            root()
            with eng.Fori(0, 3) as i:
                n.enter(i, dict(rs=2))
                root()
                root()
                n.leave(3)
            root()
            for _ in range(4):
                root()

        @block.scalar
        def _(eng):
            n = Counts()

            def split_hi(ahead=1):
                s = (n.n["unit"] + ahead) % 2
                eng.wait_ge(raw_in[s], n("unit", 8 * (ahead - s + 2), 8))
                ge(eng, acc_ready, n("tile"))
                eng.activation(w_hi[:, s, :], raw[:, s, :], ACT.Copy).then_inc(hi_split, 1)

            def load_ada():
                s = (n.n["ada"] + 1) % 2
                eng.wait_ge(ada_step, ada_count(n))
                eng.dma_start(ada_raw[:, s, :], ada[n("ada", 2 * ADA_FIRST + 1)]).then_inc(ada_in[s], 16)

            def take(s):
                eng.wait_ge(acc_ready, n("tile", 1))
                n.add("tile")
                n.add(f"set{s}")

            def square(k, first=False):
                if first:
                    eng.wait_ge(x_in[k], 16)
                    if k >= 2:
                        eng.wait_ge(sq_added, k - 1)
                else:
                    st = (n.n["tile"] + 1) % 2
                    eng.wait_ge(acc_free[st], n(f"set{st}"))
                    if k >= 2:
                        eng.wait_ge(sq_added, n("sqadd", k - 1))
                eng.activation(sq_b[k % 2], x[:, k, :], ACT.Square).then_inc(sq_done, 1)

            def spread(first=False):
                n.add("sqadd", KT - 1 if first else KT)
                n.add("aux", 2)
                eng.wait_ge(aux_ready, n("aux"))
                eng.activation(rb_b, aux[:, :], ACT.Copy).then_inc(aux_free, 1)

            def apply(g_row, shift_at):
                eng.wait_ge(gain_done, 2 * g_row + 2)
                for k in range(KT):
                    eng.wait_ge(xn_done, n("xn", k + 1))
                    if k >= 2:
                        eng.wait_ge(h_ready, n("h", k - 1))
                    eng.activation(hf_b[k % 2], xn_b[k % 2], ACT.Identity,
                                   bias=modv[:, shift_at + k:shift_at + k + 1],
                                   scale=gain[:, g_row, k:k + 1]).then_inc(hf_done, 1)
                    eng.wait_ge(hf_done, n("xn", k + 1))
                    ge(eng, acc_ready, n("tile"))
                    eng.activation(h_hi[:, k, :], hf_b[k % 2], ACT.Copy).then_inc(hhi_done, 1)
                n.add("xn", KT)
                n.add("h", KT)

            eng.wait_ge(const_in, 48)
            eng.activation(small[:, 0, :], col("c", 0, 8), ACT.Sigmoid).then_inc(c_sig, 1)
            eng.wait_ge(lb_step, 1)
            eng.activation(small[:, 2, :], small[:, 1, :], ACT.Exp).then_inc(lb_exp, 1)
            eng.dma_start(ada_raw[:, 0, :], ada[2 * ADA_FIRST]).then_inc(ada_in[0], 16)
            for k in range(KT):
                square(k, True)
            spread(True)
            n.add("aux")
            split_hi(0)
            split_hi(1)
            apply(0, SH1)

            def slot_f(tail):
                if tail:
                    split_hi()
                load_ada()
                if tail:
                    n.add("aux")
                    eng.wait_ge(aux_ready, n("aux"))
                    eng.activation(kt_b, aux[:, :], ACT.Copy).then_inc(aux_free, 1)
                    n.add("aux")
                take(n.n["tile"] % 2)
                eng.activation(f_b, acc_now(), ACT.Sigmoid).then_inc(f_raw, 1)
                eng.activation(k_b, acc_now(), ACT.Sigmoid, scale=-1.0).then_inc(acc_free[set_now()], 1)
                n.add("ada")
                n.add("unit")

            def set_now():
                return (n.n["tile"] - 1) % 2

            def acc_now():
                return acc[set_now()][:, :]

            def slot_q(tail):
                split_hi()
                load_ada()
                if tail:
                    n.add("aux")
                    eng.wait_ge(aux_ready, n("aux"))
                    eng.activation(osq_b, aux[:, :], ACT.Square).then_inc(osq_done, 1)
                take(n.n["tile"] % 2)
                eng.activation(q_b, acc_now(), ACT.Sigmoid).then_inc(q_sig, 1)
                n.add("ada")
                n.add("unit")

            def part_hi():
                e = (n.n["head"] + 1) % 2
                eng.wait_ge(aux_free, n("aux"))
                eng.activation(o_hi[:, e, :], g_b, ACT.Copy).then_inc(ohi_done, 1)

            def slot_i(tail):
                split_hi()
                load_ada()
                if tail:
                    n.add("aux")
                    part_hi()
                take(n.n["tile"] % 2)
                ge(eng, osq_summed, n("head"))
                eng.activation(vt_b, acc_now(), ACT.Copy).then_inc(acc_free[set_now()], 1)
                n.add("ada")
                n.add("unit")

            def slot_g():
                split_hi()
                load_ada()
                n.add("aux")
                eng.wait_ge(aux_ready, n("aux"))
                eng.activation(v_b, aux[:, :], ACT.Copy).then_inc(aux_free, 1)
                take(n.n["tile"] % 2)
                ge(eng, o_split, n("head"))
                eng.activation(g_b, acc_now(), ACT.Sigmoid).then_inc(g_sig, 1)
                n.add("ada")
                n.add("unit")
                n.add("head")

            def slot_m(tiles, last=False, squares=None):
                if not last:
                    split_hi()
                for d in range(tiles):
                    n.add(f"set{n.n['tile'] % 2}")
                    n.add("tile")
                    if squares is not None:
                        square(squares + d)
                n.add("unit")

            def pair(first):
                for e in range(2):
                    slot_f(not (first and e == 0))
                    slot_q(not (first and e == 0))
                    slot_i(not (first and e == 0))
                    if e == 0 and not first:
                        slot_m(4)
                        slot_m(4)
                    slot_g()

            pair(True)
            with eng.Fori(0, 3) as i:
                n.enter(i, HG_PAIR)
                pair(False)
                n.leave(3)
            n.add("aux")
            eng.wait_ge(aux_ready, n("aux"))
            eng.activation(kt_b, aux[:, :], ACT.Copy).then_inc(aux_free, 1)
            n.add("aux")
            n.add("aux")
            eng.wait_ge(aux_ready, n("aux"))
            eng.activation(osq_b, aux[:, :], ACT.Square).then_inc(osq_done, 1)
            n.add("aux")
            part_hi()
            slot_m(4, squares=0)
            slot_m(4, squares=4)

            def slot_a(ada_too, split=True):
                if split:
                    split_hi()
                if ada_too:
                    load_ada_or_stop()
                take(n.n["tile"] % 2)
                j = n.n["hid"] % 2
                ge(eng, hid_done, n("hid", -1))
                st = set_now()
                eng.activation(relu_b[j], acc_now(), ACT.Relu).then_inc(acc_free[st], 1)
                eng.wait_ge(acc_free[st], n(f"set{st}"))
                eng.activation(relu_b[j], relu_b[j], ACT.Square).then_inc(sqr_done, 1)
                eng.wait_ge(sqr_done, n("hid", 1))
                eng.activation(hid_hi[:, n.n["hid"] // 2 % 2, j, :], relu_b[j], ACT.Copy)\
                   .then_inc(hidhi_done, 1)
                n.add("hid")
                n.add("unit")

            def load_ada_or_stop():
                if n.i is not None or n.n["ada"] + 1 < 2 * (ADA_CHUNKS - ADA_FIRST):
                    load_ada()
                n.add("ada")

            def slot_b(ada_too, last=False, squares=None):
                if ada_too:
                    load_ada_or_stop()
                slot_m(4, last, squares)

            def mlp(ada_too, last_unit_follows):
                def first(g):
                    slot_a(ada_too, split=g > 0)
                    slot_a(ada_too)

                def second(g):
                    end = g == NGROUPS - 1
                    slot_b(ada_too, squares=0 if end else None)
                    if ada_too and not end:
                        n.add("aux")
                    slot_b(ada_too, last=end and not last_unit_follows, squares=4 if end else None)

                first(0)
                first(1)
                second(0)
                with eng.Fori(0, MLP_LOOP) as i:
                    n.enter(i, MLP_TWO_ADA if ada_too else MLP_TWO)
                    for g in (1, 2):
                        first(g + 1)
                        second(g)
                    n.leave(MLP_LOOP)
                second(NGROUPS - 1)
                if ada_too:
                    n.add("aux")

            spread()
            split_hi(1)
            apply(1, SH2)
            mlp(True, True)

            spread()
            split_hi(1)
            apply(2, KSH)
            for j in range(4):
                if j:
                    split_hi()
                take(n.n["tile"] % 2)
                dst = kT[:, j, :] if j < 2 else vt2_b[j - 2]
                eng.activation(dst, acc_now(), ACT.Identity, bias=col("kvb", j))\
                   .then_inc(acc_free[set_now()], 1)
                n.add("unit")
            for j in range(4):
                n.add("aux")
                eng.wait_ge(aux_ready, n("aux"))
                t, w = j // 2, j % 2
                v = (v_al, v_sh)[w]
                m = 8 - w
                eng.activation(v[:, 0:m, t * P:(t + 1) * P],
                               aux[:, 0:m * P].rearrange("p (j n) -> p j n", n=P),
                               ACT.Copy).then_inc(aux_free, 1)
            split_hi(1)
            apply(3, SH1B)

            def exps(b):
                eng.wait_ge(sm_step, 7 * b + 4)
                ge(eng, t_ready, b)
                if b % 8 == 0:
                    eng.wait_ge(pmask, b // 8 + 1)
                for j in range(8):
                    w = QCH if b % 8 == 0 and j // 2 % 2 == 0 else P
                    ins = eng.activation(p_b[:, j * P:j * P + w], lev[:, j * P:j * P + w], ACT.Exp,
                                         bias=smx[:, 2, j:j + 1], scale=SCORE_SCALE)
                ins.then_inc(p_exp, 1)
                eng.activation(smx[:, 4, :], smx[:, 3, :], ACT.Exp).then_inc(snk_exp, 1)

            def turn(b):
                eng.wait_ge(t_ready, b + 1)
                eng.activation(pt_b, aux[:, :], ACT.Copy).then_inc(pt_done, 1)

            def q_out():
                take(n.n["tile"] % 2)
                j = q_at[0]
                q_at[0] += 1
                eng.activation(qT[:, j // 4, :, j % 4, :], acc_now().rearrange("p (n q) -> p n q", q=QCH),
                               ACT.Identity, bias=col("bq", j))\
                   .then_inc(acc_free[set_now()], 1)
                n.add("unit")

            q_at = [0]
            def batch(b, following):
                turn(b)
                if following:
                    exps(b + 1)

            for j in range(4):
                if j:
                    split_hi()
                q_out()
            for j in range(4):
                split_hi()
                if j == 0:
                    exps(0)
                batch(2 * j, True)
                batch(2 * j + 1, j < 3)
                q_out()

            q_tiles = n.n["tile"]

            def o_hi_part(p):
                for k in range(4 * p, 4 * p + 4):
                    eng.wait_ge(att_done, 8 * p + 8)
                    eng.wait_ge(acc_ready, q_tiles)
                    eng.activation(h_hi[:, k, :].rearrange("p (n q) -> p n q", q=QCH), qT[:, p, :, k % 4, :],
                                   ACT.Copy).then_inc(hhi_done, 1)

            o_hi_part(0)
            for j in range(4):
                split_hi()
                if j == 0:
                    exps(8)
                batch(8 + 2 * j, True)
                batch(9 + 2 * j, j < 3)
                for _ in range(2):
                    n.add(f"set{n.n['tile'] % 2}")
                    n.add("tile")
                n.add("unit")
            o_hi_part(1)
            for j in range(4):
                slot_m(2, squares=2 * j)
            spread()
            split_hi(1)
            apply(4, SH2B)
            mlp(False, False)
            spread()

        @block.tensor
        def _(eng):
            n = Counts()

            def mm6(out, wh, wl, rh, rl, start, stop):
                for w, r, a, b in ((wh, rh, start, False), (wh, rl, False, False), (wl, rh, False, stop)):
                    for c in range(NHALF):
                        ins = eng.matmul(out[:, c * HALF:(c + 1) * HALF], w,
                                         r[:, c * HALF:(c + 1) * HALF], start=a, stop=b)
                return ins

            def unit(parts_hi, parts_lo, tiles=1, ready=None, inject=None):
                s = n.n["unit"] % 2
                eng.wait_ge(lo_split, n("unit", 1))
                kn = KT // tiles
                for d in range(tiles):
                    st = n.n["tile"] % 2
                    ge(eng, acc_free[st], n(f"set{st}"))
                    for k in range(kn):
                        sub = d * kn + k
                        if inject and sub in inject:
                            inject[sub]()
                        if ready:
                            ready(d, k)
                        at = (k * tiles + d) * P
                        ins = mm6(acc[st], w_hi[:, s, at:at + P], w_lo[:, s, at:at + P],
                                  parts_hi(k), parts_lo(k), k == 0, k == kn - 1)
                    ins.then_inc(acc_ready, 1)
                    n.add("tile")
                    n.add(f"set{st}")
                if inject and KT in inject:
                    inject[KT]()
                n.add("unit")

            def two_units():
                s = n.n["unit"] % 2
                eng.wait_ge(lo_split, n("unit", 2))
                for st in range(2):
                    ge(eng, acc_free[st], n(f"set{st}"))
                st = n.n["tile"] % 2
                for k in range(KT):
                    eng.wait_ge(h_ready, n("h", k - KT + 1))
                    at = k * P
                    for e in range(2):
                        se, te = (s + e) % 2, (st + e) % 2
                        ins = mm6(acc[te], w_hi[:, se, at:at + P], w_lo[:, se, at:at + P],
                                  h_hi_k(k), h_lo_k(k), k == 0, k == KT - 1)
                        if k == KT - 1:
                            ins.then_inc(acc_ready, 1)
                for c, m in (("tile", 2), ("unit", 2), ("set0", 1), ("set1", 1)):
                    n.add(c, m)

            def h_hi_k(k):
                return h_hi[:, k, :]

            def h_lo_k(k):
                return h_lo[:, k, :]

            def aux_take():
                ge(eng, aux_free, n("aux"))
                n.add("aux")

            def norm(first=False):
                if first:
                    for k in range(KT):
                        eng.wait_ge(sq_done, k + 1)
                        for c in range(NCH):
                            ins = eng.matmul(aux[:, c:c + 1], sq_b[k % 2][:, c * P:(c + 1) * P],
                                             ones[:, 0:1], start=k == 0 and c == 0, stop=k == KT - 1,
                                             skip_group_check=True)
                        ins.then_inc(sq_added if k < KT - 1 else aux_ready, 1)
                    n.add("sqadd", KT - 1)
                    n.add("aux")
                else:
                    eng.wait_ge(sq_added, n("sqadd", KT))
                    n.add("sqadd", KT)
                    aux_take()
                    for c in range(NCH):
                        ins = eng.matmul(aux[:, c:c + 1], sum_b[:, c * P:(c + 1) * P], ones[:, 0:1],
                                         start=True, stop=True)
                    ins.then_inc(aux_ready, 1)
                aux_take()
                for c in range(NHALF):
                    ins = eng.matmul(aux[:, c * HALF:(c + 1) * HALF], ones[:, :],
                                     diag_b[:, c * HALF:(c + 1) * HALF], start=True, stop=True)
                ins.then_inc(aux_ready, 1)

            def ada_sums(at):
                s = n.n["red"] % 2
                eng.wait_ge(ada_step, n("red", ADA_FIRST * KT + 4 * ADA_KH, 4 * ADA_KH))
                for j in range(4):
                    ins = eng.matmul(aux[:, at + j:at + j + 1], ada_acc[:, s, j * P:(j + 1) * P],
                                     ones[:, 0:1], start=True, stop=True)
                n.add("red")
                return ins

            eng.wait_ge(const_in, 48)
            eng.wait_ge(const_set, 2)
            norm(True)
            aux_take()
            eng.wait_ge(ada_step, ADA_FIRST * KT)
            for j in range(2 * ADA_FIRST):
                ins = eng.matmul(aux[:, j:j + 1], pro_acc[:, j * P:(j + 1) * P], ones[:, 0:1],
                                 start=True, stop=True)
            ins.then_inc(aux_ready, 1)
            n.add("h", KT)

            def scores(j):
                if j == 0:
                    eng.wait_ge(acc_free[1], n("set1"))
                    eng.wait_ge(gates_done, n("head", 2, 2))
                    ge(eng, lev_copied, n("head", 0, 8))
                    for c in range(NCH):
                        ins = eng.matmul(lev[:, c * P:(c + 1) * P], k_b[:, c * P:(c + 1) * P],
                                         q_b[:, c * P:(c + 1) * P], start=True, stop=True)
                else:
                    L = 2 ** (j - 1)
                    bank = (j - 1) % 2
                    eng.wait_ge(merged, n("head", j, 8))
                    eng.wait_ge(lev_copied, n("head", max(1, j - 1), 8))
                    for c in range(NCH):
                        right = halves(q_b[:, c * P:(c + 1) * P], L)[:, :, 1, :]
                        at = bank * HALF + c * 64
                        ins = eng.matmul(lev[:, at:at + 64].rearrange("p (b l) -> p b l", l=L),
                                         k_b[:, c * P:(c + 1) * P], right, start=True, stop=True)
                ins.then_inc(lev_ready, 1)

            def turn_8(src, m=NCH, first=0):
                aux_take()
                for c in range(m):
                    ins = eng.transpose(aux[:, c * P:(c + 1) * P],
                                        src[:, first + c * P:first + (c + 1) * P], ident[:, :])
                ins.then_inc(aux_ready, 1)

            def turn_v():
                eng.wait_ge(acc_free[0], n("set0"))
                turn_8(vt_b)

            def turn_k():
                eng.wait_ge(merged, n("head", 0, 8))
                turn_8(k_b)

            def updates():
                aux_take()
                for c in range(NCH - 1):
                    eng.matmul(aux[:, c * P:(c + 1) * P], kt_b[:, c * P:(c + 1) * P],
                               v_b[:, c * P:(c + 1) * P], start=True, stop=True)
                ada_sums(T - 4).then_inc(aux_ready, 1)

            def head_out():
                eng.wait_ge(lev_copied, n("head", 0, 8))
                aux_take()
                for c in range(NCH):
                    ins = eng.matmul(aux[:, c * P:(c + 1) * P], a_b[:, c * P:(c + 1) * P],
                                     v_b[:, c * P:(c + 1) * P], start=True, stop=c == 0)
                    if c:
                        ins = eng.matmul(aux[:, c * P:(c + 1) * P], q_b[:, c * P:(c + 1) * P],
                                         s_b[:, (c - 1) * P:c * P], start=False, stop=True)
                ins.then_inc(aux_ready, 1)

            def turn_o():
                turn_8(on_b)

            def out_pair(first_wait):
                def ready(d, k):
                    if d == 0 and k == 0:
                        eng.wait_ge(o_split, first_wait)
                for _ in range(2):
                    unit(lambda k: o_hi[:, k, :], lambda k: o_lo[:, k, :], 4, ready)

            def pair(first):
                for e in range(2):
                    if first and e == 0:
                        two_units()
                    else:
                        unit(h_hi_k, h_lo_k, 1, None, {2: turn_k, 5: updates})
                        unit(h_hi_k, h_lo_k, 1, None, {2: head_out})
                    levels = {3: lambda: scores(0), 5: lambda: scores(1), 7: lambda: scores(2)}
                    if not (first and e == 0):
                        levels[1] = turn_o
                    unit(h_hi_k, h_lo_k, 1, None, levels)
                    if e == 0 and not first:
                        out_pair(n("head"))
                    unit(h_hi_k, h_lo_k, 1, None,
                         {0: lambda: scores(3), 1: turn_v, 2: lambda: scores(4),
                          4: lambda: scores(5), 6: lambda: scores(6), 7: lambda: scores(7)})
                    n.add("head")
                    n.add("ada", 4)

            pair(True)
            with eng.Fori(0, 3) as i:
                n.enter(i, HG_PAIR)
                pair(False)
                n.leave(3)
            turn_k()
            updates()
            head_out()
            turn_o()
            out_pair(HEADS)

            def mlp(ada_too):
                def first(g):
                    if g == 0:
                        two_units()
                    for _ in range(GROUP):
                        if g:
                            unit(h_hi_k, h_lo_k)
                        n.add("hid")
                        if ada_too:
                            n.add("ada")

                def second(par, behind, sums):
                    for un in range(2):
                        def ready(d, k):
                            if un == 0 and d == 0:
                                eng.wait_ge(hid_done, n("hid", k + 1 - GROUP - behind))
                        unit(lambda k: hid_hi[:, par, k, :], lambda k: hid_lo[:, par, k, :], 4, ready,
                             {2: sums} if sums and un == 0 else None)
                        if ada_too:
                            n.add("ada")

                def sums():
                    aux_take()
                    ada_sums(0).then_inc(aux_ready, 1)

                s = sums if ada_too else None
                first(0)
                first(1)
                second(0, GROUP, s)
                with eng.Fori(0, MLP_LOOP) as i:
                    n.enter(i, MLP_TWO_ADA if ada_too else MLP_TWO)
                    for g in (1, 2):
                        first(g + 1)
                        second(g % 2, GROUP, s)
                    n.leave(MLP_LOOP)
                second((NGROUPS - 1) % 2, 0, None)
                if ada_too:
                    sums()

            norm()
            n.add("h", KT)
            mlp(True)

            norm()
            n.add("h", KT)
            two_units()
            unit(h_hi_k, h_lo_k)
            unit(h_hi_k, h_lo_k)
            for j in range(4):
                t, w = j // 2, j % 2
                st = (n.n["tile"] + t) % 2
                eng.wait_ge(acc_free[st], n(f"set{st}"))
                turn_8(vt2_b[t], 8 - w, w * QCH)
            n.add("h", KT)
            two_units()
            unit(h_hi_k, h_lo_k)
            unit(h_hi_k, h_lo_k)
            q_sets = [[n.n["set0"] + 2 * p, n.n["set1"] + 2 * p] for p in range(2)]
            v_turned = n("aux")

            def att_scores(b):
                p, m = b // 8, b % 8
                if m == 0:
                    for st in range(2):
                        eng.wait_ge(acc_free[st], q_sets[p][st])
                if b:
                    eng.wait_ge(p_exp, b)
                for a in range(2):
                    for c in range(2):
                        n0 = 2 * m + c
                        key = QCH * max(n0 - 1, 0)
                        for gp in range(2):
                            at = a * HALF + c * 256 + gp * P
                            ins = eng.matmul(lev[:, at:at + P],
                                             qT[64 * a:64 * a + 64, p, n0, 2 * gp:2 * gp + 2, :]
                                             .rearrange("p g q -> p (g q)"),
                                             kT[64 * a:64 * a + 64, p, key:key + P],
                                             start=True, stop=True)
                ins.then_inc(s_ready, 1)

            def att_turn(b):
                eng.wait_ge(p_done, b + 1)
                if b == 0:
                    eng.wait_ge(aux_free, v_turned)
                else:
                    eng.wait_ge(att_done, b)
                for j in range(8):
                    ins = eng.transpose(aux[:, j * P:(j + 1) * P], p_b[:, j * P:(j + 1) * P], ident[:, :])
                ins.then_inc(t_ready, 1)

            def att_out(b):
                p, m = b // 8, b % 8
                eng.wait_ge(pt_done, b + 1)
                for a in range(2):
                    for c in range(2):
                        v = v_al[:, m, :] if c or not m else v_sh[:, m - 1, :]
                        hd = (2 * p + a) * 64
                        ins = eng.matmul(aux[64 * a:64 * a + 64, c * 256:(c + 1) * 256],
                                         v[:, hd:hd + 64],
                                         pt_b[:, a * HALF + c * 256:a * HALF + (c + 1) * 256],
                                         start=True, stop=True)
                ins.then_inc(o_ready, 1)

            def two_batches(b):
                if b % 8 == 0:
                    return {0: lambda: att_scores(b), 3: lambda: att_scores(b + 1),
                            4: lambda: att_turn(b), 6: lambda: att_out(b),
                            7: lambda: att_scores(b + 2), 8: lambda: att_turn(b + 1)}
                steps = {0: lambda: (att_out(b - 1), att_scores(b + 1)), 2: lambda: att_turn(b),
                         4: lambda: att_out(b), 6: lambda: att_turn(b + 1)}
                steps.update({5: lambda: att_scores(b + 2)} if b % 8 < 6 else
                             {8: lambda: att_out(b + 1)})
                return steps

            for j in range(4):
                unit(h_hi_k, h_lo_k, 1, None, two_batches(2 * j))

            def o_ready_k(p):
                def ready(d, k):
                    if d == 0:
                        eng.wait_ge(h_ready, n("h", 4 * p + k + 1))
                return ready

            for p in range(2):
                for j in range(4):
                    unit(lambda k: h_hi[:, 4 * p + k, :], lambda k: h_lo[:, 4 * p + k, :], 2,
                         o_ready_k(p), two_batches(8 + 2 * j) if p == 0 else None)
            n.add("h", KT)

            norm()
            n.add("h", KT)
            mlp(False)
            norm()

        @block.vector
        def _(eng):
            n = Counts()

            def split_lo(ahead=1):
                s = (n.n["unit"] + ahead) % 2
                eng.wait_ge(hi_split, n("unit", ahead + 1))
                eng.tensor_tensor(w_lo[:, s, :], raw[:, s, :], w_hi[:, s, :].bitcast(f32), ALU.subtract)\
                   .then_inc(lo_split, 1)

            def take(wait=True):
                if wait:
                    eng.wait_ge(acc_ready, n("tile", 1))
                s = n.n["tile"] % 2
                n.add("tile")
                n.add(f"set{s}")
                return s

            def ada_unit():
                i = n.n["ada"] % 4
                s, g = n.n["ada"] % 2, n.n["ada"] // 4 % 2
                eng.wait_ge(ada_in[s], n("ada", 8 * (2 - s), 8))
                dst = ada_acc[:, g, (i // 2) * ADA_N:(i // 2 + 1) * ADA_N]
                for k in range(ADA_KH):
                    kk = (i % 2) * ADA_KH + k
                    src = ada_raw[:, s, k * ADA_N:(k + 1) * ADA_N]
                    cv = cact[:, kk:kk + 1]
                    if kk == 0:
                        ins = eng.tensor_scalar(dst, src, cv, None, ALU.mult)
                    else:
                        eng.wait_ge(ada_step, ada_steps(k))
                        ins = eng.scalar_tensor_tensor(out=dst, in0=src, scalar=cv, in1=dst,
                                                       op0=ALU.mult, op1=ALU.add)
                    ins.then_inc(ada_step, 1)
                n.add("ada")

            def ada_steps(k):
                return n("ada", ADA_FIRST * KT + k, ADA_KH)

            def mod_cols(at):
                ins = eng.tensor_tensor(modv[:, bass.ds(n("red", 16, 4), 4)], aux[:, at:at + 4],
                                        vecs[:, bass.ds(n("red", 16 + COLS["adab"], 4), 4)], ALU.add)
                n.add("red")
                return ins

            def stream(gate_at, d):
                s = take()
                eng.scalar_tensor_tensor(out=x[:, d, :], in0=acc[s][:, :],
                                         scalar=modv[:, gate_at + d:gate_at + d + 1], in1=x[:, d, :],
                                         op0=ALU.mult, op1=ALU.add)\
                   .then_inc(acc_free[s], 1)

            def add_square(k):
                if k < 1:
                    return
                eng.wait_ge(sq_done, n("sqadd", k + 2))
                if k == 1:
                    eng.tensor_tensor(sum_b, sq_b[0], sq_b[1], ALU.add).then_inc(sq_added, 2)
                else:
                    eng.wait_ge(sq_added, n("sqadd", k))
                    eng.tensor_tensor(sum_b, sum_b, sq_b[k % 2], ALU.add).then_inc(sq_added, 1)

            def norm(first=False):
                if not first:
                    add_square(KT - 1)
                n.add("sqadd", KT - 1 if first else KT)
                n.add("aux")
                s = n.n["rs"] % 2
                eng.wait_ge(aux_ready, n("aux"))
                eng.tensor_scalar(ms[:, s, :], aux[:, 0:8], 1.0 / D, EPS, ALU.mult, ALU.add)\
                   .then_inc(ms_ready, 1)
                eng.wait_ge(rstd_ready, n("rs", 1))
                n.add("rs")
                eng.tensor_tensor(diag_b.rearrange("p (c t) -> p c t", t=P),
                                  ident[:, :].rearrange("p (o t) -> p o t", o=1).broadcast_to([P, NCH, P]),
                                  rstd[:, s, :].rearrange("p (c o) -> p c o", o=1).broadcast_to([P, NCH, P]),
                                  ALU.mult).then_inc(aux_free, 1)
                n.add("aux")

            def rb_ready():
                eng.wait_ge(aux_free, n("aux"))

            def gains(row, name, scale_at):
                eng.tensor_scalar(small[:, 4 + row, :], modv[:, scale_at:scale_at + 8], 1.0, None, ALU.add)\
                   .then_inc(gain_done, 1)
                eng.wait_ge(gain_done, 2 * row + 1)
                eng.tensor_tensor(gain[:, row, :], small[:, 4 + row, :], col(name, 0, 8), ALU.mult)\
                   .then_inc(gain_done, 1)

            def apply():
                for k in range(KT + 1):
                    if k < KT:
                        if k >= 2:
                            eng.wait_ge(hf_done, n("xn", k - 1))
                        eng.tensor_tensor(xn_b[k % 2], x[:, k, :], rb_b, ALU.mult).then_inc(xn_done, 1)
                    if k:
                        j = k - 1
                        eng.wait_ge(hhi_done, n("h", j + 1))
                        eng.tensor_tensor(h_lo[:, j, :], hf_b[j % 2], h_hi[:, j, :].bitcast(f32),
                                          ALU.subtract).then_inc(h_ready, 1)
                n.add("h", KT)
                n.add("xn", KT)

            eng.wait_ge(const_in, 48)
            eng.wait_ge(c_sig, 1)
            eng.tensor_tensor(cact[:, :], col("c", 0, 8), small[:, 0, :], ALU.mult).then_inc(c_act_done, 1)
            eng.tensor_tensor(small[:, 1, :], col("gamma", 0, 8), col("gamma", 0, 8), ALU.subtract)\
               .then_inc(lb_step, 1)
            eng.wait_ge(lb_exp, 1)
            eng.reciprocal(small[:, 3, :], small[:, 2, :]).then_inc(lb_step, 1)
            eng.wait_ge(lb_step, 2)
            eng.tensor_tensor(small[:, 3, :], small[:, 3, :], small[:, 2, :], ALU.mult).then_inc(lb_step, 1)
            eng.wait_ge(lb_step, 3)
            eng.tensor_tensor(lb[:, :], small[:, 3, :], small[:, 3, :], ALU.subtract).then_inc(lb_step, 1)
            eng.wait_ge(lb_step, 4)
            eng.tensor_scalar(lb[:, :], lb[:, :], 0.0, None, ALU.max).then_inc(lb_step, 1)
            eng.wait_ge(lb_step, 5)
            eng.tensor_scalar(omlb[:, :], lb[:, :], -1.0, 1.0, ALU.mult, ALU.add).then_inc(lb_step, 1)
            eng.wait_ge(c_act_done, 1)
            for j in range(ADA_FIRST):
                eng.wait_ge(pro_in[j % 4], 16 * (j // 4 + 1))
                dst = pro_acc[:, j * ADA_N:(j + 1) * ADA_N]
                for k in range(KT):
                    src = pro_b[j % 4][:, k * ADA_N:(k + 1) * ADA_N]
                    if k == 0:
                        ins = eng.tensor_scalar(dst, src, cact[:, 0:1], None, ALU.mult)
                    else:
                        eng.wait_ge(ada_step, j * KT + k)
                        ins = eng.scalar_tensor_tensor(out=dst, in0=src, scalar=cact[:, k:k + 1],
                                                       in1=dst, op0=ALU.mult, op1=ALU.add)
                    ins.then_inc(ada_step, 1)
            norm(True)
            rb_ready()
            n.add("aux")
            eng.wait_ge(aux_ready, n("aux"))
            eng.tensor_tensor(modv[:, 0:16], aux[:, 0:16], col("adab", 0, 16), ALU.add)\
               .then_inc(aux_free, 1)
            eng.wait_ge(aux_free, n("aux"))
            gains(0, "mix0", SC1)
            split_lo(0)
            split_lo(1)
            eng.wait_ge(masks_set, LEVELS + 1)
            apply()
            eng.memset(a_b, 0.0).then_inc(a_zero, 1)

            def merge(j):
                if j == 1:
                    eng.wait_ge(lev_ready, n("head", 1, 8))
                    eng.tensor_tensor(q_b, q_b, f_b, ALU.mult).then_inc(merged, 1)
                    return
                L = 2 ** (j - 2)
                eng.wait_ge(lev_ready, n("head", j, 8))
                eng.wait_ge(merged, n("head", j - 1, 8))
                eng.wait_ge(lev_copied, n("head", j - 1, 8))
                fl = fprod(L).rearrange("p (b two) -> p b two", two=2)
                even, odd = fl[:, :, 0:1], fl[:, :, 1:2]
                nb = T // (2 * L)
                eng.tensor_tensor(fprod(2 * L).rearrange("p (b o) -> p b o", o=1), even, odd, ALU.mult)
                qr, kl = halves(q_b, L)[:, :, 1, :], halves(k_b, L)[:, :, 0, :]
                eng.tensor_tensor(qr, qr, even.broadcast_to([P, nb, L]), ALU.mult)
                eng.tensor_tensor(kl, kl, odd.broadcast_to([P, nb, L]), ALU.mult).then_inc(merged, 1)

            def keep(j):
                if j == 0:
                    eng.copy_predicated(a_b, masks[:, LEVELS * HALF:], lev[:, :]).then_inc(lev_copied, 1)
                    return
                L = 2 ** (j - 1)
                bank = (j - 1) % 2
                eng.copy_predicated(
                    halves(a_b, L)[:, :, 1, :],
                    masks[:, (j - 1) * HALF:j * HALF].rearrange("p (b l) -> p b l", l=L),
                    lev[:, bank * HALF:(bank + 1) * HALF].rearrange("p (b l) -> p b l", l=L))\
                   .then_inc(lev_copied, 1)

            def states():
                n.add("aux")
                eng.wait_ge(aux_ready, n("aux"))
                mod_cols(T - 4).then_inc(mod_done, 1)
                decay = fprod(P)
                eng.tensor_copy(s_b[:, 0:P], aux[:, 0:P]).then_inc(state_done, 1)
                last = NCH - 2
                for c in range(1, last + 1):
                    eng.wait_ge(state_done, n("head", c - last, last))
                    eng.scalar_tensor_tensor(out=s_b[:, c * P:(c + 1) * P],
                                                   in0=s_b[:, (c - 1) * P:c * P],
                                                   scalar=decay[:, c:c + 1],
                                                   in1=aux[:, c * P:(c + 1) * P],
                                                   op0=ALU.mult, op1=ALU.add)\
                       .then_inc(aux_free if c == last else state_done, 1)

            def norm_out():
                n.add("aux")
                s = n.n["rs"] % 2
                eng.wait_ge(osq_done, n("head"))
                eng.tensor_reduce(small[:, 15, :], osq_b.rearrange("p (c v) -> p c v", v=P), AX.X, ALU.add)\
                   .then_inc(osq_summed, 1)
                eng.wait_ge(osq_summed, n("head"))
                eng.tensor_scalar(ms[:, s, :], small[:, 15, :], 1.0 / P, EPS, ALU.mult, ALU.add)\
                   .then_inc(ms_ready, 1)
                eng.wait_ge(rstd_ready, n("rs", 1))
                n.add("rs")
                eng.tensor_tensor(on_b.rearrange("p (c v) -> p c v", v=P),
                                  aux[:, :].rearrange("p (c v) -> p c v", v=P),
                                  rstd[:, s, :].rearrange("p (c o) -> p c o", o=1).broadcast_to([P, NCH, P]),
                                  ALU.mult).then_inc(aux_free, 1)

            def gate_out():
                n.add("aux")
                eng.wait_ge(acc_free[1], n("set1"))
                eng.wait_ge(aux_ready, n("aux"))
                eng.scalar_tensor_tensor(out=g_b, in0=aux[:, :], scalar=col("gnorm"), in1=g_b,
                                         op0=ALU.mult, op1=ALU.mult)\
                   .then_inc(aux_free, 1)

            def part_lo():
                e = (n.n["head"] + 1) % 2
                eng.wait_ge(ohi_done, n("head"))
                eng.tensor_tensor(o_lo[:, e, :], g_b, o_hi[:, e, :].bitcast(f32), ALU.subtract)\
                   .then_inc(o_split, 1)

            def slot_f(tail):
                if tail:
                    split_lo()
                ada_unit()
                if tail:
                    n.add("aux")
                    states()
                s = take()
                hd = n("head")
                eng.wait_ge(f_raw, n("head", 1))
                eng.tensor_scalar(f_b, f_b, omlb[:, bass.ds(hd, 1)], lb[:, bass.ds(hd, 1)],
                                  ALU.mult, ALU.add).then_inc(gates_done, 1)
                eng.wait_ge(acc_free[s], n(f"set{s}"))
                eng.tensor_scalar(k_b, k_b, omlb[:, bass.ds(hd, 1)], None, ALU.mult)\
                   .then_inc(gates_done, 1)
                n.add("unit")

            def slot_q(tail):
                split_lo()
                ada_unit()
                if tail:
                    norm_out()
                s = take()
                eng.wait_ge(q_sig, n("head", 1))
                eng.tensor_tensor(q_b, q_b, acc[s][:, :], ALU.mult)\
                   .then_inc(acc_free[s], 1)
                n.add("unit")

            def slot_i(tail):
                split_lo()
                ada_unit()
                if tail:
                    gate_out()
                else:
                    eng.wait_ge(a_zero, 1)
                eng.wait_ge(gates_done, n("head", 2, 2))
                eng.wait_ge(acc_free[1], n("set1"))
                for j in range(3):
                    merge(j + 1)
                    keep(j)
                    if tail and j == 0:
                        part_lo()
                take(False)
                n.add("unit")

            def out_units():
                for un in range(2):
                    for d in range(4):
                        stream(G1, 4 * un + d)
                        if d == 0:
                            split_lo()
                    n.add("unit")

            def slot_g():
                split_lo()
                ada_unit()
                n.add("aux")
                for j in range(3, 8):
                    merge(j + 1)
                    keep(j)
                s = take()
                eng.wait_ge(g_sig, n("head", 1))
                eng.tensor_tensor(g_b, g_b, acc[s][:, :], ALU.mult)\
                   .then_inc(acc_free[s], 1)
                n.add("unit")
                n.add("head")

            def pair(first):
                for e in range(2):
                    tail = not (first and e == 0)
                    slot_f(tail)
                    slot_q(tail)
                    slot_i(tail)
                    if e == 0 and not first:
                        out_units()
                    slot_g()

            pair(True)
            with eng.Fori(0, 3) as i:
                n.enter(i, HG_PAIR)
                pair(False)
                n.leave(3)
            n.add("aux")
            states()
            norm_out()
            gate_out()
            part_lo()
            for un in range(2):
                for d in range(4):
                    stream(G1, 4 * un + d)
                    if d == 0:
                        split_lo()
                    add_square(4 * un + d - 1)
                n.add("unit")

            def mlp(ada_too, gate_at, unit_follows):
                def hidden_lo():
                    j, par = n.n["hid"] % 2, n.n["hid"] // 2 % 2
                    eng.wait_ge(hidhi_done, n("hid", 1))
                    eng.tensor_tensor(hid_lo[:, par, j, :], relu_b[j],
                                      hid_hi[:, par, j, :].bitcast(f32), ALU.subtract)\
                       .then_inc(hid_done, 1)
                    n.add("hid")

                def first(g):
                    for un in range(GROUP):
                        if g or un:
                            split_lo()
                        if ada_too:
                            ada_unit()
                        take(False)
                        if g == 0 or un == 0:
                            hidden_lo()
                        n.add("unit")

                def second(g, sums):
                    end = g == NGROUPS - 1
                    for un in range(2):
                        for d in range(4):
                            stream(gate_at, 4 * un + d)
                            if end:
                                add_square(4 * un + d - 1)
                            elif un == 0 and d == 0:
                                hidden_lo()
                            if d == 1 - un and (un == 0 or not end or unit_follows):
                                split_lo()
                            if d == 2 - un and ada_too:
                                ada_unit()
                            if un == 0 and d == 2 and sums:
                                group_cols()
                        n.add("unit")

                def group_cols():
                    n.add("aux")
                    eng.wait_ge(aux_ready, n("aux"))
                    mod_cols(0).then_inc(aux_free, 1)

                first(0)
                first(1)
                second(0, ada_too)
                with eng.Fori(0, MLP_LOOP) as i:
                    n.enter(i, MLP_TWO_ADA if ada_too else MLP_TWO)
                    for g in (1, 2):
                        first(g + 1)
                        second(g, ada_too)
                    n.leave(MLP_LOOP)
                second(NGROUPS - 1, False)
                if ada_too:
                    group_cols()

            eng.wait_ge(mod_done, HEADS)
            gains(1, "mlp0", SC2)
            norm()
            split_lo()
            rb_ready()
            apply()
            mlp(True, G2, True)

            eng.wait_ge(aux_free, n("aux"))
            gains(2, "kvn", KSC)
            gains(3, "mix1", SC1B)
            norm()
            split_lo()
            rb_ready()
            apply()
            for j in range(4):
                if j:
                    split_lo()
                take(False)
                n.add("unit")
            n.add("aux", 4)
            split_lo()
            apply()

            def blocks(buf):
                return buf.rearrange("p (j n) -> p j n", n=P)

            def maxima(b):
                eng.wait_ge(s_ready, b + 1)
                if b % 8 == 0:
                    for a in range(2):
                        for c in range(2):
                            j = 4 * a + 2 * c
                            w = P if c else QCH
                            ins = eng.tensor_reduce(smx[:, 0, j:j + 2],
                                                    blocks(lev[:, :])[:, j:j + 2, 0:w], AX.X, ALU.max)
                    ge(eng, t_ready, b)
                    for a in range(2):
                        zero = eng.memset(blocks(p_b)[:, 4 * a:4 * a + 2, QCH:P], 0.0)
                    zero.then_inc(pmask, 1)
                else:
                    ins = eng.tensor_reduce(smx[:, 0, :], blocks(lev[:, :]), AX.X, ALU.max)
                ins.then_inc(sm_step, 1)
                sink = col("sink", 8 * (b // 8), 8)
                eng.wait_ge(sm_step, 7 * b + 1)
                eng.scalar_tensor_tensor(out=smx[:, 1, :], in0=smx[:, 0, :], scalar=SCORE_SCALE,
                                         in1=sink, op0=ALU.mult, op1=ALU.max).then_inc(sm_step, 1)
                eng.wait_ge(sm_step, 7 * b + 2)
                eng.tensor_scalar(smx[:, 2, :], smx[:, 1, :], -1.0, None, ALU.mult).then_inc(sm_step, 1)
                eng.tensor_tensor(smx[:, 3, :], sink, smx[:, 1, :], ALU.subtract).then_inc(sm_step, 1)

            def normalise(b):
                eng.wait_ge(p_exp, b + 1)
                eng.tensor_reduce(smx[:, 5, :], blocks(p_b), AX.X, ALU.add).then_inc(sm_step, 1)
                eng.wait_ge(snk_exp, b + 1)
                eng.wait_ge(sm_step, 7 * b + 5)
                eng.tensor_tensor(smx[:, 5, :], smx[:, 5, :], smx[:, 4, :], ALU.add).then_inc(sm_step, 1)
                eng.wait_ge(sm_step, 7 * b + 6)
                eng.reciprocal(smx[:, 1, :], smx[:, 5, :]).then_inc(sm_step, 1)
                eng.wait_ge(sm_step, 7 * b + 7)
                eng.tensor_tensor(blocks(p_b), blocks(p_b),
                                  smx[:, 1, :].rearrange("p (j o) -> p j o", o=1).broadcast_to([P, 8, P]),
                                  ALU.mult).then_inc(p_done, 1)

            def heads_out(b):
                p, m = b // 8, b % 8
                eng.wait_ge(o_ready, b + 1)
                eng.tensor_copy(qT[:, p, 2 * m:2 * m + 2, :, :].rearrange("p c g q -> p (c g q)"),
                                aux[:, 0:HALF]).then_inc(att_done, 1)

            def o_lo_part(p):
                for k in range(4 * p, 4 * p + 4):
                    eng.wait_ge(hhi_done, n("h", k + 1))
                    eng.tensor_tensor(h_lo[:, k, :].rearrange("p (n q) -> p n q", q=QCH),
                                      qT[:, p, :, k % 4, :],
                                      h_hi[:, k, :].bitcast(f32).rearrange("p (n q) -> p n q", q=QCH),
                                      ALU.subtract).then_inc(h_ready, 1)

            def batches(b, early=None, late=None):
                if b % 8 == 0:
                    split_lo()
                    maxima(b)
                else:
                    heads_out(b - 1)
                normalise(b)
                if early is not None:
                    stream(G1B, early)
                maxima(b + 1)
                if b % 8:
                    split_lo()
                heads_out(b)
                if late is not None:
                    stream(G1B, late)
                normalise(b + 1)
                if b % 8 < 6:
                    maxima(b + 2)
                else:
                    heads_out(b + 1)

            for j in range(4):
                if j:
                    split_lo()
                take(False)
                n.add("unit")
            for j in range(4):
                batches(2 * j)
                take(False)
                n.add("unit")
            o_lo_part(0)
            for j in range(4):
                batches(8 + 2 * j, 2 * j - 1 if j else None, 2 * j)
                n.add("unit")
            stream(G1B, KT - 1)
            o_lo_part(1)
            for j in range(4):
                for d in range(2):
                    stream(G1B, 2 * j + d)
                    if d == 0:
                        split_lo()
                    add_square(2 * j + d - 1)
                n.add("unit")
            n.add("h", KT)

            gains(4, "mlp1", SC2B)
            norm()
            split_lo()
            rb_ready()
            apply()
            mlp(False, G2B, False)
            norm()
            rb_ready()
            for k in range(KT):
                eng.scalar_tensor_tensor(out=out_b[k], in0=x[:, k, :], scalar=col("fin", k), in1=rb_b,
                                         op0=ALU.mult, op1=ALU.mult).then_inc(fin_done, 1)


def kernel(**inputs):
    import numpy as np
    import concourse.bacc as bacc
    from concourse.bass_utils import run_bass_kernel_spmd

    a = {k: np.asarray(v) for k, v in inputs.items()}
    f32 = mybir.dt.float32

    def square_units(w):
        k, m = w.shape
        return w.reshape(KT, P, m // P, P).transpose(2, 1, 0, 3).reshape(m // P, P, UNIT)

    def wide_units(w, kn):
        r, m = w.shape
        wide = UNIT // kn
        return w.reshape(r // (kn * P), kn, P, m // wide, wide).transpose(0, 3, 2, 1, 4)\
                .reshape(-1, P, UNIT)

    def by_pairs(w):
        return w.reshape((2, 2, 4, 64) + w.shape[1:]).transpose((0, 2, 1, 3) + tuple(range(4, 3 + w.ndim)))\
                .reshape(w.shape)

    w_in, w_out = a["hg_w_in"][0], a["hg_w_out"][0]
    uq, uf, ui, ug = (square_units(w_in[:, i * D:(i + 1) * D]) for i in range(4))
    uo = wide_units(w_out, 2)
    units = []
    for pr in range(HEADS // 2):
        for e in range(2):
            hd = 2 * pr + e
            units += [uf[hd], uq[hd], ui[hd]]
            if e == 0 and pr:
                units += [uo[2 * pr - 2], uo[2 * pr - 1]]
            units += [ug[hd]]
    units += [uo[6], uo[7]]

    def mlp_units(l):
        u1, u2 = square_units(a["mlp_w1"][l]), wide_units(a["mlp_w2"][l], GROUP)
        out = [u1[0], u1[1]]
        for g in range(NGROUPS):
            if g + 1 < NGROUPS:
                out += [u1[2 * g + 2], u1[2 * g + 3]]
            out += [u2[2 * g], u2[2 * g + 1]]
        return out

    units += mlp_units(0)
    units += list(square_units(a["kv_w"]))
    units += list(square_units(by_pairs(a["sw_w_q"][0].T).T))
    units += list(wide_units(by_pairs(a["sw_w_o"][0]), 4))
    units += mlp_units(1)
    weights = np.stack(units)
    assert weights.shape == (N_UNITS, P, UNIT)

    ada = np.concatenate([a["ada_w"][0], a["kv_ada_w"], a["ada_w"][1]], axis=1)
    ada = ada.reshape(2, ADA_KH, P, ADA_CHUNKS, ADA_N).transpose(3, 0, 2, 1, 4)\
             .reshape(2 * ADA_CHUNKS, P, ADA_KH * ADA_N)

    def columns(v):
        return v.reshape(-1, P).T

    sinks = a["sw_sinks"][0].reshape(2, 2, 2, 2)
    sink = np.empty((P, 2, 2, 2, 2), sinks.dtype)
    for g2 in range(2):
        sink[64 * g2:64 * g2 + 64] = sinks[None, :, :, None, :, g2]
    parts = dict(c=columns(a["c"][0]), mix0=columns(a["norm_mix"][0]), mix1=columns(a["norm_mix"][1]),
                 mlp0=columns(a["norm_mlp"][0]), mlp1=columns(a["norm_mlp"][1]),
                 kvn=columns(a["kv_norm"]), fin=columns(a["final_norm"]),
                 gnorm=columns(a["hg_g_norm"][0]), gamma=columns(a["hg_lb_gamma"][0]),
                 kvb=columns(a["kv_b"]), bq=columns(by_pairs(a["sw_b_q"][0])),
                 sink=sink.reshape(P, 16),
                 adab=columns(np.concatenate([a["ada_b"][0], a["kv_ada_b"], a["ada_b"][1]])))
    cols = np.ascontiguousarray(np.concatenate([parts[k] for k in COLS], axis=1))

    key, query = np.arange(P)[:, None], np.arange(P)[None, :]
    masks = []
    for j in range(LEVELS):
        L = 2 ** j
        pairs = (key // (2 * L) == query // (2 * L)) & (key // L % 2 == 0)
        masks.append(pairs[:, query[0] // L % 2 == 1])
    masks = np.concatenate(masks + [key == query], axis=1).astype(np.float32)

    arrays = {
        "xT": np.ascontiguousarray(a["x"][0].T).reshape(KT, P, T),
        "weights": weights, "ada": np.ascontiguousarray(ada), "cols": cols,
        "ident": np.eye(P, dtype=np.float32), "masks": masks,
    }
    nc = bacc.Bacc("TRN2", target_bir_lowering=False, num_devices=1)
    aps = [nc.dram_tensor("in_" + k, v.shape, mybir.dt.from_np(v.dtype), kind="ExternalInput").ap()
           for k, v in arrays.items()]
    out = nc.dram_tensor("outT", (KT, P, T), f32, kind="ExternalOutput").ap()
    build(nc, *aps, out)
    r = run_bass_kernel_spmd(nc, [{"in_" + k: v for k, v in arrays.items()}], core_ids=[0])
    return np.ascontiguousarray(r.results[0]["outT"].reshape(D, T).T)[None]
```

```python
import concourse.bass as bass
from concourse import mybir
from contextlib import ExitStack

P = 128
T = 1024
D = 1024
KT = D // P
HALF = 512
NHALF = T // HALF
HEADS = 8
NCH = T // P
LEVELS = 7
DEPTH = 2
D_FF = 4096
GROUP = 2
NGROUPS = D_FF // P // GROUP
KV_TILES = 2
QCH = 64
EPS = 1e-6
UNIT = 1024
ADA_N = 256
ADA_KH = 4
ADA_CHUNKS = (6 * D * DEPTH + 2 * D) // ADA_N
ADA_FIRST = 2 * D // ADA_N
PRO_STEPS = ADA_FIRST // 2 * KT
SCORE_SCALE = 64 ** -0.5

U_HGRN = HEADS * 4 + HEADS
U_MLP = 2 * D_FF // P
U_ATT = 4 + 8 + 8
N_UNITS = U_HGRN + DEPTH * U_MLP + U_ATT

COLS = {}
_at = 0
for _name, _n in (("c", 8), ("mix0", 8), ("mix1", 8), ("mlp0", 8), ("mlp1", 8), ("kvn", 8),
                  ("fin", 8), ("gnorm", 1), ("gamma", 8), ("kvb", 4), ("bq", 8), ("sink", 16),
                  ("adab", 112)):
    COLS[_name] = _at
    _at += _n
N_COLS = _at
SH1, SC1, G1, SH2, SC2, G2, KSH, KSC, SH1B, SC1B, G1B, SH2B, SC2B, G2B = (8 * i for i in range(14))

HG_PAIR = dict(unit=10, tile=16, set0=8, set1=8, aux=10, head=2, ada=8, red=2, rs=2)
MLP_TWO = dict(unit=8, tile=20, set0=10, set1=10, hid=4)
MLP_TWO_ADA = dict(MLP_TWO, aux=2, ada=8, red=2)


def ada_count(n):
    return n("ada", PRO_STEPS, ADA_KH)


class Counts:

    def __init__(self):
        self.n = dict.fromkeys(("unit", "tile", "set0", "set1", "aux", "head", "ada", "red",
                                "rs", "hid", "sqadd", "xn", "h", "norm"), 0)
        self.i, self.per, self.start = None, {}, None

    def __call__(self, name, plus=0, times=1, over=1):
        v = self.n[name] // over * times + plus
        per = self.per.get(name, 0)
        return v + self.i * (per // over * times) if per else v

    def add(self, name, k=1):
        self.n[name] += k

    def enter(self, i, per):
        self.i, self.per, self.start = i, per, dict(self.n)

    def leave(self, times):
        for k, v in self.n.items():
            if v != self.start[k]:
                assert v - self.start[k] == self.per[k], (k, v - self.start[k])
                self.n[k] = self.start[k] + times * self.per[k]
        self.i, self.per = None, {}


def build(nc, xT, weights, ada, cols, ident_in, masks_in, outT):
    f32, f32r, u8 = mybir.dt.float32, mybir.dt.float32r, mybir.dt.uint8
    ALU, ACT, AX = mybir.AluOpType, mybir.ActivationFunctionType, mybir.AxisListType
    ctx = ExitStack()
    with ctx:
        def sb(name, shape, dt=f32):
            return ctx.enter_context(nc.sbuf_tensor(name, shape, dt))

        def sem(name):
            return ctx.enter_context(nc.semaphore(name))

        x = sb("x", [P, KT, T])
        h_hi = sb("h_hi", [P, KT, T], f32r)
        h_lo = sb("h_lo", [P, KT, T], f32r)
        raw = sb("raw", [P, 2, UNIT])
        w_hi = sb("w_hi", [P, 2, UNIT], f32r)
        w_lo = sb("w_lo", [P, 2, UNIT], f32r)
        ada_raw = sb("ada_raw", [P, 2, ADA_KH * ADA_N])
        ada_acc = sb("ada_acc", [P, 2, 2 * ADA_N])
        ident = sb("ident", [P, P])
        ones = sb("ones", [P, P])
        masks = sb("masks", [P, LEVELS * HALF + T], u8)
        vecs = sb("vecs", [P, N_COLS])
        modv = sb("modv", [P, 14 * 8])
        cact = sb("cact", [P, 8])
        lb = sb("lb", [P, 8])
        omlb = sb("omlb", [P, 8])
        small = sb("small", [P, 16, 8])
        gain = sb("gain", [P, 5, 8])
        ms = sb("ms", [P, 2, 8])
        rstd = sb("rstd", [P, 2, 8])
        mhalf = sb("mhalf", [P, 8])
        smx = sb("smx", [P, 6, 8])

        zone = sb("zone", [P, 16 * T])
        zone_at = nc.sbuf_base - 4 * 16 * T

        def over(name, tile, shape, dt=f32):
            return nc.alloc_sbuf_tensor_at(name, shape, dt, offset=zone_at + tile * 4 * T)

        def z(tile, n=1):
            return zone[:, tile * T:(tile + n) * T]

        q_b, k_b, f_b, fp_b, vt_b, v_b, a_b, kt_b, s_b, g_b, on_b = (z(i) for i in range(11))
        osq_b = vt_b
        o_hi = over("o_hi", 11, [P, 2, T], f32r)
        o_lo = over("o_lo", 13, [P, 2, T], f32r)
        sq_b = [z(9), z(10)]
        xn_b = sq_b
        sum_b, rb_b, diag_b = z(8), z(13), z(12)
        hf_b = [z(11), z(12)]
        pro_b = [z(2 * i, 2) for i in range(4)]
        pro_acc = z(14, 2)
        stage_b = z(11)[:, 0:LEVELS * 64 + P]
        hid_hi = over("hid_hi", 0, [P, 2, GROUP, T], f32r)
        hid_lo = over("hid_lo", 4, [P, 2, GROUP, T], f32r)
        relu_b = [z(14), z(15)]
        kT = zone[:, 0:2 * T].rearrange("p (t n) -> p t n", t=2)
        v_al = zone[:, 2 * T:4 * T].rearrange("p (j n) -> p j n", n=256)
        v_sh = zone[:, 4 * T:6 * T].rearrange("p (j n) -> p j n", n=256)
        vt2_b = [z(6), z(7)]
        p_b, pt_b = z(6), z(7)
        out_b = [z(k) for k in range(KT)]
        qT = zone[:, 8 * T:16 * T].rearrange("p (a n g q) -> p a n g q", a=2, g=4, q=QCH)

        acc = [ctx.enter_context(nc.psum_tensor(f"acc{s}", [P, T], f32)) for s in range(2)]
        lev = ctx.enter_context(nc.psum_tensor("lev", [P, T], f32))
        aux = ctx.enter_context(nc.psum_tensor("aux", [P, T], f32))

        h_read = sem("h_read")
        vecs_in, const_in = sem("vecs_in"), sem("const_in")
        pro_read = sem("pro_read")
        x_in = [sem(f"x_in{k}") for k in range(KT)]
        const_set = sem("const_set")
        masks_set = sem("masks_set")
        raw_in = [sem(f"raw_in{s}") for s in range(2)]
        hi_split = sem("hi_split")
        lo_split = sem("lo_split")
        acc_ready = sem("acc_ready")
        acc_free = [sem(f"acc_free{s}") for s in range(2)]
        aux_ready, aux_free = sem("aux_ready"), sem("aux_free")
        pro_in = [sem(f"pro_in{s}") for s in range(4)]
        ada_in = [sem(f"ada_in{s}") for s in range(2)]
        ada_step = sem("ada_step")
        mod_done = sem("mod_done")
        c_sig, c_act_done, lb_exp = sem("c_sig"), sem("c_act_done"), sem("lb_exp")
        lb_step = sem("lb_step")
        gain_done = sem("gain_done")
        sq_done, sq_added = sem("sq_done"), sem("sq_added")
        ms_step, ms_ready, rstd_ready = sem("ms_step"), sem("ms_ready"), sem("rstd_ready")
        xn_done, hf_done, hhi_done, h_ready = sem("xn_done"), sem("hf_done"), sem("hhi_done"), sem("h_ready")
        f_raw, gates_done = sem("f_raw"), sem("gates_done")
        q_sig, g_sig = sem("q_sig"), sem("g_sig")
        lev_ready, lev_copied, merged = sem("lev_ready"), sem("lev_copied"), sem("merged")
        state_done, a_zero = sem("state_done"), sem("a_zero")
        osq_done, osq_summed = sem("osq_done"), sem("osq_summed")
        ohi_done, o_split = sem("ohi_done"), sem("o_split")
        sqr_done, hidhi_done, hid_done = (sem(n) for n in ("sqr_done", "hidhi_done", "hid_done"))
        s_ready, p_exp, p_done, t_ready, pt_done, o_ready = (
            sem(n) for n in ("s_ready", "p_exp", "p_done", "t_ready", "pt_done", "o_ready"))
        sm_step, snk_exp, att_done, pmask = sem("sm_step"), sem("snk_exp"), sem("att_done"), sem("pmask")
        fin_done, out_done = sem("fin_done"), sem("out_done")

        block = ctx.enter_context(nc.Block())

        def col(name, i=0, n=1):
            return vecs[:, COLS[name] + i:COLS[name] + i + n]

        def ge(eng, s, v):
            if not isinstance(v, int) or v > 0:
                eng.wait_ge(s, v)

        def half(c):
            return slice(c * HALF, (c + 1) * HALF)

        def halves(buf, L):
            return buf.rearrange("p (b two l) -> p b two l", two=2, l=L)

        FP_AT = {1: None}
        at = 0
        for j in range(1, LEVELS + 1):
            FP_AT[2 ** j] = at
            at += T >> j

        def fprod(L):
            return f_b if L == 1 else fp_b[:, FP_AT[L]:FP_AT[L] + T // L]

        MLP_LOOP = (NGROUPS - 2) // 2

        @block.sync
        def _(eng):
            eng.dma_start(vecs[:, :], cols).then_inc(vecs_in, 16)
            for j in range(ADA_FIRST):
                if j == 2:
                    eng.dma_start(ident[:, :], ident_in).then_inc(const_in, 16)
                    eng.dma_start(stage_b, masks_in).then_inc(const_in, 16)
                if j == 4:
                    for u in range(2):
                        eng.dma_start(raw[:, u, :], weights[u]).then_inc(raw_in[u], 16)
                if j >= 4:
                    if j % 2 == 0:
                        eng.wait_ge(ada_step, KT * ((j - 4) // 2 + 1))
                    else:
                        eng.wait_ge(pro_read, (j - 4) // 2 + 1)
                eng.dma_start(pro_b[j % 4].rearrange("p (h n) -> p h n", h=2),
                              ada[2 * j:2 * j + 2].rearrange("h p n -> p h n"))\
                   .then_inc(pro_in[j % 4], 16)
            for k in range(KT):
                eng.dma_start(x[:, k, :], xT[k]).then_inc(x_in[k], 16)

            with eng.Fori(1, N_UNITS // 2) as i:
                for s in range(2):
                    eng.wait_ge(lo_split, i * 2 + (s - 1))
                    eng.dma_start(raw[:, s, :], weights[i * 2 + s]).then_inc(raw_in[s], 16)

            for c in range(NHALF):
                for k in range(KT):
                    eng.wait_ge(fin_done, c * KT + k + 1)
                    eng.dma_start(outT[k][:, half(c)], out_b[k][:, half(c)]).then_inc(out_done, 16)
            eng.wait_ge(out_done, 16 * KT * NHALF)

        @block.gpsimd
        def _(eng):
            eng.memset(ones[:, :], 1.0).then_inc(const_set, 1)
            eng.memset(mhalf[:, :], -0.5).then_inc(const_set, 1)
            eng.wait_ge(const_in, 32)
            for j in range(LEVELS + 1):
                w = 64 if j < LEVELS else P
                at = j * HALF
                eng.tensor_copy(masks[:, at:at + NCH * w].rearrange("p (c m) -> p c m", c=NCH),
                                stage_b[:, j * 64:j * 64 + w].rearrange("p (o m) -> p o m", o=1)
                                .broadcast_to([P, NCH, w])).then_inc(masks_set, 1)
            eng.wait_ge(ada_step, PRO_STEPS)
            eng.wait_ge(aux_ready, 1)
            eng.memset(a_b, 0.0).then_inc(a_zero, 1)
            n = Counts()

            def root(first=0, width=8):
                s, w = n.n["rs"] % 2, slice(first, first + width)
                eng.wait_ge(ms_ready, n("rs", 1))
                eng.tensor_tensor(rstd[:, s, w], ms[:, s, w], mhalf[:, w], ALU.pow)\
                   .then_inc(rstd_ready, 1)
                n.add("rs")

            eng.wait_ge(const_set, 2)
            root()
            root()
            with eng.Fori(0, 3) as i:
                n.enter(i, dict(rs=2))
                root()
                root()
                n.leave(3)
            root()
            for _ in range(4):
                for c in range(NHALF):
                    root(c * 4, 4)

        @block.scalar
        def _(eng):
            n = Counts()

            def split_hi(ahead=1):
                s = (n.n["unit"] + ahead) % 2
                eng.wait_ge(raw_in[s], n("unit", 8 * (ahead - s + 2), 8))
                ge(eng, acc_ready, n("tile"))
                eng.activation(w_hi[:, s, :], raw[:, s, :], ACT.Copy).then_inc(hi_split, 1)

            def load_ada():
                s = (n.n["ada"] + 1) % 2
                eng.wait_ge(ada_step, ada_count(n))
                eng.dma_start(ada_raw[:, s, :], ada[n("ada", 2 * ADA_FIRST + 1)]).then_inc(ada_in[s], 16)

            def take(s):
                eng.wait_ge(acc_ready, n("tile", 1))
                n.add("tile")
                n.add(f"set{s}")

            def square(k, c=None):
                w = half(c) if c is not None else slice(0, T)
                if c is None:
                    eng.wait_ge(x_in[k], 16)
                else:
                    st = (n.n["tile"] + 1) % 2
                    eng.wait_ge(acc_free[st], n(f"set{st}"))
                if k >= 2:
                    eng.wait_ge(sq_added, n("sqadd", k - 1))
                eng.activation(sq_b[k % 2][:, w], x[:, k, w], ACT.Square).then_inc(sq_done, 1)

            def spread(c=None):
                w = half(c) if c is not None else slice(0, T)
                n.add("aux", 2)
                eng.wait_ge(aux_ready, n("aux"))
                eng.activation(rb_b[:, w], aux[:, w], ACT.Copy).then_inc(aux_free, 1)

            def modulate(i, g_row, shift_at, free, c=None):
                k = i % KT
                w = half(c) if c is not None else slice(0, T)
                eng.wait_ge(xn_done, n("xn", i + 1))
                if i == 0:
                    eng.wait_ge(gain_done, 2 * g_row + 2)
                if k >= 2:
                    eng.wait_ge(h_ready, n("h", i - 1))
                eng.activation(hf_b[k % 2][:, w], xn_b[k % 2][:, w], ACT.Identity,
                               bias=modv[:, shift_at + k:shift_at + k + 1],
                               scale=gain[:, g_row, k:k + 1]).then_inc(hf_done, 1)
                eng.wait_ge(hf_done, n("xn", i + 1))
                ge(eng, *free)
                eng.activation(h_hi[:, k, w], hf_b[k % 2][:, w], ACT.Copy).then_inc(hhi_done, 1)

            def normed(steps):
                n.add("xn", steps)
                n.add("h", steps)

            def last_two(load, end):
                split_hi()
                for c in range(NHALF):
                    for d in range(KT):
                        if load and c == 0 and d % 4 == 0:
                            load()
                        n.add(f"set{n.n['tile'] % 2}")
                        n.add("tile")
                        if c == 1 and d == KT - 1 and not end:
                            split_hi(3)
                        square(d, c)
                        if c == 1 and d == 3 and not end:
                            split_hi(2)

                        yield c, d
                    n.add("sqadd", KT)

            def norm(end, rows=None, load=None, columns=False):
                read = None
                for c, d in last_two(load, end):
                    if c == 0 and d == KT - 1:
                        read = n("tile")
                    if c == 1 and d == 4:
                        if columns:
                            n.add("aux")
                        spread(0)
                    if c == 1 and d in (4, 5) and rows:
                        modulate(d - 4, *rows, (acc_ready, read), 0)
                n.add("unit", 2)
                if end:
                    spread(1)
                    return
                for i in range(2, KT):
                    modulate(i, *rows, (acc_ready, read), 0)
                spread(1)
                for i in range(KT, 2 * KT):
                    modulate(i, *rows, (acc_ready, n("tile")), 1)
                normed(2 * KT)

            eng.wait_ge(vecs_in, 16)
            eng.activation(small[:, 0, :], col("c", 0, 8), ACT.Sigmoid).then_inc(c_sig, 1)
            eng.wait_ge(lb_step, 1)
            eng.activation(small[:, 2, :], small[:, 1, :], ACT.Exp).then_inc(lb_exp, 1)
            eng.dma_start(ada_raw[:, 0, :], ada[2 * ADA_FIRST]).then_inc(ada_in[0], 16)
            split_hi(0)
            split_hi(1)
            for k in range(KT):
                square(k)
            n.add("sqadd", KT)
            n.add("aux")
            spread()
            for k in range(KT):
                modulate(k, 0, SH1, (acc_ready, 0))
            normed(KT)

            def slot_f(tail):
                if tail:
                    split_hi()
                load_ada()
                if tail:
                    n.add("aux")
                    eng.wait_ge(aux_ready, n("aux"))
                    eng.activation(kt_b, aux[:, :], ACT.Copy).then_inc(aux_free, 1)
                    n.add("aux")
                take(n.n["tile"] % 2)
                if not tail:
                    split_hi(2)
                eng.activation(f_b, acc_now(), ACT.Sigmoid).then_inc(f_raw, 1)
                eng.activation(k_b, acc_now(), ACT.Sigmoid, scale=-1.0).then_inc(acc_free[set_now()], 1)
                n.add("ada")
                n.add("unit")

            def set_now():
                return (n.n["tile"] - 1) % 2

            def acc_now():
                return acc[set_now()][:, :]

            def slot_q(tail):
                if tail:
                    split_hi()
                load_ada()
                if tail:
                    n.add("aux")
                    eng.wait_ge(aux_ready, n("aux"))
                    eng.activation(osq_b, aux[:, :], ACT.Square).then_inc(osq_done, 1)
                take(n.n["tile"] % 2)
                eng.activation(q_b, acc_now(), ACT.Sigmoid).then_inc(q_sig, 1)
                n.add("ada")
                n.add("unit")

            def part_hi():
                e = (n.n["head"] + 1) % 2
                eng.wait_ge(aux_free, n("aux"))
                eng.activation(o_hi[:, e, :], g_b, ACT.Copy).then_inc(ohi_done, 1)

            def slot_i(tail):
                split_hi()
                load_ada()
                if tail:
                    n.add("aux")
                    part_hi()
                take(n.n["tile"] % 2)
                ge(eng, osq_summed, n("head"))
                eng.activation(vt_b, acc_now(), ACT.Copy).then_inc(acc_free[set_now()], 1)
                n.add("ada")
                n.add("unit")

            def slot_g():
                split_hi()
                load_ada()
                n.add("aux")
                eng.wait_ge(aux_ready, n("aux"))
                eng.activation(v_b, aux[:, :], ACT.Copy).then_inc(aux_free, 1)
                take(n.n["tile"] % 2)
                ge(eng, o_split, n("head"))
                eng.activation(g_b, acc_now(), ACT.Sigmoid).then_inc(g_sig, 1)
                n.add("ada")
                n.add("unit")
                n.add("head")

            def slot_m(tiles):
                split_hi()
                for d in range(tiles):
                    n.add(f"set{n.n['tile'] % 2}")
                    n.add("tile")
                n.add("unit")

            def pair(first):
                for e in range(2):
                    slot_f(not (first and e == 0))
                    slot_q(not (first and e == 0))
                    slot_i(not (first and e == 0))
                    if e == 0 and not first:
                        slot_m(4)
                        slot_m(4)
                    slot_g()

            pair(True)
            with eng.Fori(0, 3) as i:
                n.enter(i, HG_PAIR)
                pair(False)
                n.leave(3)
            n.add("aux")
            eng.wait_ge(aux_ready, n("aux"))
            eng.activation(kt_b, aux[:, :], ACT.Copy).then_inc(aux_free, 1)
            n.add("aux")
            n.add("aux")
            eng.wait_ge(aux_ready, n("aux"))
            eng.activation(osq_b, aux[:, :], ACT.Square).then_inc(osq_done, 1)
            n.add("aux")
            part_hi()
            norm(False, (1, SH2))

            def slot_a(ada_too, un, g):
                if g > 0:
                    split_hi()
                if ada_too:
                    load_ada_or_stop()
                take(n.n["tile"] % 2)
                if g == 0 and un == 0:
                    split_hi(2)
                j = n.n["hid"] % 2
                ge(eng, hid_done, n("hid", -1))
                st = set_now()
                eng.activation(relu_b[j], acc_now(), ACT.Relu).then_inc(acc_free[st], 1)
                eng.wait_ge(acc_free[st], n(f"set{st}"))
                eng.activation(relu_b[j], relu_b[j], ACT.Square).then_inc(sqr_done, 1)
                eng.wait_ge(sqr_done, n("hid", 1))
                eng.activation(hid_hi[:, n.n["hid"] // 2 % 2, j, :], relu_b[j], ACT.Copy)\
                   .then_inc(hidhi_done, 1)
                n.add("hid")
                n.add("unit")

            def load_ada_or_stop():
                if n.i is not None or n.n["ada"] + 1 < 2 * (ADA_CHUNKS - ADA_FIRST):
                    load_ada()
                n.add("ada")

            def slot_b(ada_too):
                if ada_too:
                    load_ada_or_stop()
                slot_m(4)

            def mlp(ada_too, end, rows=None):
                def first(g):
                    for un in range(GROUP):
                        slot_a(ada_too, un, g)

                def second(g):
                    slot_b(ada_too)
                    if ada_too:
                        n.add("aux")
                    slot_b(ada_too)

                first(0)
                first(1)
                second(0)
                with eng.Fori(0, MLP_LOOP) as i:
                    n.enter(i, MLP_TWO_ADA if ada_too else MLP_TWO)
                    for g in (1, 2):
                        first(g + 1)
                        second(g)
                    n.leave(MLP_LOOP)
                norm(end, rows, load_ada_or_stop if ada_too else None, ada_too)

            mlp(True, False, (2, KSH))

            for j in range(4):
                if j > 1:
                    split_hi()
                if j == 3:
                    for k in range(5):
                        modulate(k, 3, SH1B, (h_read, k + 1))
                take(n.n["tile"] % 2)
                if j == 0:
                    split_hi(2)
                dst = kT[:, j, :] if j < 2 else vt2_b[j - 2]
                eng.activation(dst, acc_now(), ACT.Identity, bias=col("kvb", j))\
                   .then_inc(acc_free[set_now()], 1)
                n.add("unit")
            split_hi(1)
            for k in range(5, KT):
                modulate(k, 3, SH1B, (acc_ready, n("tile")))
            normed(KT)

            def turn_v(t, w):
                n.add("aux")
                eng.wait_ge(aux_ready, n("aux"))
                v = (v_al, v_sh)[w]
                m = 8 - w
                eng.activation(v[:, 0:m, t * P:(t + 1) * P],
                               aux[:, 0:m * P].rearrange("p (j n) -> p j n", n=P),
                               ACT.Copy).then_inc(aux_free, 1)

            def exps(b):
                eng.wait_ge(sm_step, 7 * b + 4)
                ge(eng, t_ready, b)
                if b % 8 == 0:
                    eng.wait_ge(pmask, b // 8 + 1)
                for j in range(8):
                    w = QCH if b % 8 == 0 and j // 2 % 2 == 0 else P
                    ins = eng.activation(p_b[:, j * P:j * P + w], lev[:, j * P:j * P + w], ACT.Exp,
                                         bias=smx[:, 2, j:j + 1], scale=SCORE_SCALE)
                ins.then_inc(p_exp, 1)
                eng.activation(smx[:, 4, :], smx[:, 3, :], ACT.Exp).then_inc(snk_exp, 1)

            def turn(b):
                eng.wait_ge(t_ready, b + 1)
                eng.activation(pt_b, aux[:, :], ACT.Copy).then_inc(pt_done, 1)

            def q_out():
                take(n.n["tile"] % 2)
                j = q_at[0]
                q_at[0] += 1
                eng.activation(qT[:, j // 4, :, j % 4, :], acc_now().rearrange("p (n q) -> p n q", q=QCH),
                               ACT.Identity, bias=col("bq", j))\
                   .then_inc(acc_free[set_now()], 1)
                n.add("unit")

            q_at = [0]
            def batch(b, following):
                turn(b)
                if following:
                    exps(b + 1)

            for j in range(4):
                if j:
                    split_hi()
                if j in (1, 2):
                    turn_v(j - 1, 0)
                    turn_v(j - 1, 1)
                q_out()
            for j in range(4):
                split_hi()
                if j == 0:
                    exps(0)
                batch(2 * j, True)
                batch(2 * j + 1, j < 3)
                q_out()

            q_tiles = n.n["tile"]

            def o_hi_part(p):
                for k in range(4 * p, 4 * p + 4):
                    eng.wait_ge(att_done, 8 * p + 8)
                    eng.wait_ge(acc_ready, q_tiles)
                    eng.activation(h_hi[:, k, :].rearrange("p (n q) -> p n q", q=QCH), qT[:, p, :, k % 4, :],
                                   ACT.Copy).then_inc(hhi_done, 1)

            o_hi_part(0)
            for j in range(4):
                split_hi()
                if j == 0:
                    exps(8)
                batch(8 + 2 * j, True)
                batch(9 + 2 * j, j < 3)
                for _ in range(2):
                    n.add(f"set{n.n['tile'] % 2}")
                    n.add("tile")
                n.add("unit")
            o_hi_part(1)
            slot_m(4)
            slot_m(4)
            n.add("h", KT)
            norm(False, (4, SH2B))
            mlp(False, True)

        @block.tensor
        def _(eng):
            n = Counts()

            def mm6(out, wh, wl, rh, rl, start, stop):
                for w, r, a, b in ((wh, rh, start, False), (wh, rl, False, False), (wl, rh, False, stop)):
                    for c in range(NHALF):
                        ins = eng.matmul(out[:, c * HALF:(c + 1) * HALF], w,
                                         r[:, c * HALF:(c + 1) * HALF], start=a, stop=b)
                return ins

            def mm3(out, wh, wl, rh, rl, start, stop, c):
                w = half(c)
                eng.matmul(out[:, w], wh, rh[:, w], start=start, stop=False)
                eng.matmul(out[:, w], wh, rl[:, w], start=False, stop=False)
                return eng.matmul(out[:, w], wl, rh[:, w], start=False, stop=stop)

            def unit(parts_hi, parts_lo, tiles=1, ready=None, inject=None, release=False):
                s = n.n["unit"] % 2
                eng.wait_ge(lo_split, n("unit", 1))
                kn = KT // tiles
                for d in range(tiles):
                    st = n.n["tile"] % 2
                    ge(eng, acc_free[st], n(f"set{st}"))
                    for k in range(kn):
                        sub = d * kn + k
                        if inject and sub in inject:
                            inject[sub]()
                        if ready:
                            ready(d, k)
                        at = (k * tiles + d) * P
                        ins = mm6(acc[st], w_hi[:, s, at:at + P], w_lo[:, s, at:at + P],
                                  parts_hi(k), parts_lo(k), k == 0, k == kn - 1)
                        if release and k < kn - 1:
                            ins.then_inc(h_read, 1)
                    ins.then_inc(acc_ready, 1)
                    n.add("tile")
                    n.add(f"set{st}")
                if inject and KT in inject:
                    inject[KT]()
                n.add("unit")

            def two_units(in_halves, inject=None):
                s = n.n["unit"] % 2
                eng.wait_ge(lo_split, n("unit", 2))
                for st in range(2):
                    ge(eng, acc_free[st], n(f"set{st}"))
                st = n.n["tile"] % 2
                parts = NHALF if in_halves else 1
                for c in range(parts):
                    for k in range(KT):
                        if inject and c == 0 and k in inject:
                            inject[k]()
                        eng.wait_ge(h_ready, n("h", c * KT + k + 1))
                        at = k * P
                        for e in range(2):
                            se, te = (s + e) % 2, (st + e) % 2
                            wh, wl = w_hi[:, se, at:at + P], w_lo[:, se, at:at + P]
                            if in_halves:
                                ins = mm3(acc[te], wh, wl, h_hi_k(k), h_lo_k(k), k == 0, k == KT - 1, c)
                            else:
                                ins = mm6(acc[te], wh, wl, h_hi_k(k), h_lo_k(k), k == 0, k == KT - 1)
                            if k == KT - 1 and c == parts - 1:
                                ins.then_inc(acc_ready, 1)
                for name, m in (("tile", 2), ("unit", 2), ("set0", 1), ("set1", 1), ("h", parts * KT)):
                    n.add(name, m)

            def last_two(parts_hi, parts_lo, ready=None, columns=None):
                s = n.n["unit"] % 2
                for c in range(NHALF):
                    for d in range(KT):
                        un = d // 4
                        if c == 0 and d % 4 == 0:
                            eng.wait_ge(lo_split, n("unit", un + 1))
                        if c == 1 and d == 0 and columns:
                            columns()
                        if c == 1 and d == 2:
                            square_sums(0)
                        if c == 1 and d == 5:
                            spread(0)
                        st = n.n["tile"] % 2
                        ge(eng, acc_free[st], n(f"set{st}"))
                        su = (s + un) % 2
                        for k in range(2):
                            if ready and c == 0 and d == 0:
                                ready(k)
                            at = (k * 4 + d % 4) * P
                            ins = mm3(acc[st], w_hi[:, su, at:at + P], w_lo[:, su, at:at + P],
                                      parts_hi(k), parts_lo(k), k == 0, k == 1, c)
                        ins.then_inc(acc_ready, 1)
                        n.add("tile")
                        n.add(f"set{st}")
                n.add("unit", 2)

            def h_hi_k(k):
                return h_hi[:, k, :]

            def h_lo_k(k):
                return h_lo[:, k, :]

            def aux_take():
                ge(eng, aux_free, n("aux"))
                n.add("aux")

            def square_sums(c):
                eng.wait_ge(sq_added, n("sqadd", KT))
                n.add("sqadd", KT)
                aux_take()
                for j in range(NCH // 2):
                    at = c * HALF + j
                    ins = eng.matmul(aux[:, at:at + 1], sum_b[:, c * HALF + j * P:c * HALF + (j + 1) * P],
                                     ones[:, 0:1], start=True, stop=True)
                ins.then_inc(aux_ready, 1)

            def spread(c):
                aux_take()
                eng.matmul(aux[:, half(c)], ones[:, :], diag_b[:, half(c)], start=True, stop=True)\
                   .then_inc(aux_ready, 1)

            second_half = {2: lambda: square_sums(1), 6: lambda: spread(1)}

            def ada_sums(at):
                s = n.n["red"] % 2
                eng.wait_ge(ada_step, n("red", PRO_STEPS + 4 * ADA_KH, 4 * ADA_KH))
                for j in range(4):
                    ins = eng.matmul(aux[:, at + j:at + j + 1], ada_acc[:, s, j * P:(j + 1) * P],
                                     ones[:, 0:1], start=True, stop=True)
                n.add("red")
                return ins

            eng.wait_ge(const_set, 2)
            eng.wait_ge(c_act_done, 1)
            aux_take()
            for j in range(ADA_FIRST):
                if j % 2 == 0:
                    eng.wait_ge(ada_step, KT * (j // 2 + 1))
                    for at in (2 * j, 2 * j + 1):
                        ins = eng.matmul(aux[:, at:at + 1], pro_acc[:, at * P:(at + 1) * P],
                                         ones[:, 0:1], start=True, stop=True)
                else:
                    eng.wait_ge(pro_in[j % 4], 16 * (j // 4 + 1))
                    for m in range(2):
                        at = 2 * j + m
                        for k in range(KT):
                            w = k * ADA_N + m * P
                            ins = eng.matmul(aux[:, at:at + 1], pro_b[j % 4][:, w:w + P],
                                             cact[:, k:k + 1], start=k == 0, stop=k == KT - 1)
                    ins.then_inc(pro_read if j < ADA_FIRST - 1 else aux_ready, 1)
            aux_take()
            eng.wait_ge(sq_added, KT)
            n.add("sqadd", KT)
            for c in range(NCH):
                ins = eng.matmul(aux[:, c:c + 1], sum_b[:, c * P:(c + 1) * P], ones[:, 0:1],
                                 start=True, stop=True)
            ins.then_inc(aux_ready, 1)
            aux_take()
            for c in range(NHALF):
                ins = eng.matmul(aux[:, half(c)], ones[:, :], diag_b[:, half(c)], start=True, stop=True)
            ins.then_inc(aux_ready, 1)

            eng.wait_ge(const_in, 32)

            def scores(j):
                if j == 0:
                    eng.wait_ge(acc_free[1], n("set1"))
                    eng.wait_ge(gates_done, n("head", 2, 2))
                    ge(eng, lev_copied, n("head", 0, 8))
                    for c in range(NCH):
                        ins = eng.matmul(lev[:, c * P:(c + 1) * P], k_b[:, c * P:(c + 1) * P],
                                         q_b[:, c * P:(c + 1) * P], start=True, stop=True)
                else:
                    L = 2 ** (j - 1)
                    bank = (j - 1) % 2
                    eng.wait_ge(merged, n("head", j, 8))
                    eng.wait_ge(lev_copied, n("head", max(1, j - 1), 8))
                    for c in range(NCH):
                        right = halves(q_b[:, c * P:(c + 1) * P], L)[:, :, 1, :]
                        at = bank * HALF + c * 64
                        ins = eng.matmul(lev[:, at:at + 64].rearrange("p (b l) -> p b l", l=L),
                                         k_b[:, c * P:(c + 1) * P], right, start=True, stop=True)
                ins.then_inc(lev_ready, 1)

            def turn_8(src, m=NCH, first=0):
                aux_take()
                for c in range(m):
                    ins = eng.transpose(aux[:, c * P:(c + 1) * P],
                                        src[:, first + c * P:first + (c + 1) * P], ident[:, :])
                ins.then_inc(aux_ready, 1)

            def turn_v():
                eng.wait_ge(acc_free[0], n("set0"))
                turn_8(vt_b)

            def turn_k():
                eng.wait_ge(merged, n("head", 0, 8))
                turn_8(k_b)

            def updates():
                aux_take()
                for c in range(NCH - 1):
                    eng.matmul(aux[:, c * P:(c + 1) * P], kt_b[:, c * P:(c + 1) * P],
                               v_b[:, c * P:(c + 1) * P], start=True, stop=True)
                ada_sums(T - 4).then_inc(aux_ready, 1)

            def head_out():
                eng.wait_ge(lev_copied, n("head", 0, 8))
                aux_take()
                for c in range(NCH):
                    ins = eng.matmul(aux[:, c * P:(c + 1) * P], a_b[:, c * P:(c + 1) * P],
                                     v_b[:, c * P:(c + 1) * P], start=True, stop=c == 0)
                    if c:
                        ins = eng.matmul(aux[:, c * P:(c + 1) * P], q_b[:, c * P:(c + 1) * P],
                                         s_b[:, (c - 1) * P:c * P], start=False, stop=True)
                ins.then_inc(aux_ready, 1)

            def turn_o():
                turn_8(on_b)

            def out_pair(first_wait):
                def ready(d, k):
                    if d == 0 and k == 0:
                        eng.wait_ge(o_split, first_wait)
                for _ in range(2):
                    unit(lambda k: o_hi[:, k, :], lambda k: o_lo[:, k, :], 4, ready)

            def pair(first):
                for e in range(2):
                    if first and e == 0:
                        two_units(False)
                    else:
                        unit(h_hi_k, h_lo_k, 1, None, {2: turn_k, 5: updates})
                        unit(h_hi_k, h_lo_k, 1, None, {2: head_out})
                    levels = {3: lambda: scores(0), 5: lambda: scores(1), 7: lambda: scores(2)}
                    if not (first and e == 0):
                        levels[1] = turn_o
                    unit(h_hi_k, h_lo_k, 1, None, levels)
                    if e == 0 and not first:
                        out_pair(n("head"))
                    unit(h_hi_k, h_lo_k, 1, None,
                         {0: lambda: scores(3), 1: turn_v, 2: lambda: scores(4),
                          4: lambda: scores(5), 6: lambda: scores(6), 7: lambda: scores(7)})
                    n.add("head")
                    n.add("ada", 4)

            pair(True)
            with eng.Fori(0, 3) as i:
                n.enter(i, HG_PAIR)
                pair(False)
                n.leave(3)
            turn_k()
            updates()
            head_out()
            turn_o()
            eng.wait_ge(o_split, HEADS)
            last_two(lambda k: o_hi[:, k, :], lambda k: o_lo[:, k, :])

            def mlp(ada_too):
                def first(g):
                    if g == 0:
                        two_units(True, second_half)
                    for _ in range(GROUP):
                        if g:
                            unit(h_hi_k, h_lo_k)
                        n.add("hid")
                        if ada_too:
                            n.add("ada")

                def second(par, behind, sums):
                    for un in range(2):
                        def ready(d, k):
                            if un == 0 and d == 0:
                                eng.wait_ge(hid_done, n("hid", k + 1 - GROUP - behind))
                        unit(lambda k: hid_hi[:, par, k, :], lambda k: hid_lo[:, par, k, :], 4, ready,
                             {2: sums} if sums and un == 0 else None)
                        if ada_too:
                            n.add("ada")

                def sums():
                    aux_take()
                    ada_sums(0).then_inc(aux_ready, 1)

                s = sums if ada_too else None
                first(0)
                first(1)
                second(0, GROUP, s)
                with eng.Fori(0, MLP_LOOP) as i:
                    n.enter(i, MLP_TWO_ADA if ada_too else MLP_TWO)
                    for g in (1, 2):
                        first(g + 1)
                        second(g % 2, GROUP, s)
                    n.leave(MLP_LOOP)
                par = (NGROUPS - 1) % 2
                last_two(lambda k: hid_hi[:, par, k, :], lambda k: hid_lo[:, par, k, :],
                         lambda k: eng.wait_ge(hid_done, n("hid", k + 1 - GROUP)), s)
                if ada_too:
                    n.add("ada", 2)

            mlp(True)

            two_units(True, second_half)
            unit(h_hi_k, h_lo_k)
            unit(h_hi_k, h_lo_k, release=True)
            v_sets = n.n["set0"], n.n["set1"]

            def turn_values(t, w):
                for st in range(2):
                    eng.wait_ge(acc_free[st], v_sets[st])
                turn_8(vt2_b[t], 8 - w, w * QCH)

            unit(h_hi_k, h_lo_k, 1, lambda d, k: eng.wait_ge(h_ready, n("h", k + 1)))
            n.add("h", KT)
            for t in range(KV_TILES):
                unit(h_hi_k, h_lo_k, 1, None,
                     {2: lambda: turn_values(t, 0), 5: lambda: turn_values(t, 1)})
            unit(h_hi_k, h_lo_k)
            q_sets = [[n.n["set0"] + 2 * p, n.n["set1"] + 2 * p] for p in range(2)]
            v_turned = n("aux")

            def att_scores(b):
                p, m = b // 8, b % 8
                if m == 0:
                    for st in range(2):
                        eng.wait_ge(acc_free[st], q_sets[p][st])
                if b:
                    eng.wait_ge(p_exp, b)
                for a in range(2):
                    for c in range(2):
                        n0 = 2 * m + c
                        key = QCH * max(n0 - 1, 0)
                        for gp in range(2):
                            at = a * HALF + c * 256 + gp * P
                            ins = eng.matmul(lev[:, at:at + P],
                                             qT[64 * a:64 * a + 64, p, n0, 2 * gp:2 * gp + 2, :]
                                             .rearrange("p g q -> p (g q)"),
                                             kT[64 * a:64 * a + 64, p, key:key + P],
                                             start=True, stop=True)
                ins.then_inc(s_ready, 1)

            def att_turn(b):
                eng.wait_ge(p_done, b + 1)
                if b == 0:
                    eng.wait_ge(aux_free, v_turned)
                else:
                    eng.wait_ge(att_done, b)
                for j in range(8):
                    ins = eng.transpose(aux[:, j * P:(j + 1) * P], p_b[:, j * P:(j + 1) * P], ident[:, :])
                ins.then_inc(t_ready, 1)

            def att_out(b):
                p, m = b // 8, b % 8
                eng.wait_ge(pt_done, b + 1)
                for a in range(2):
                    for c in range(2):
                        v = v_al[:, m, :] if c or not m else v_sh[:, m - 1, :]
                        hd = (2 * p + a) * 64
                        ins = eng.matmul(aux[64 * a:64 * a + 64, c * 256:(c + 1) * 256],
                                         v[:, hd:hd + 64],
                                         pt_b[:, a * HALF + c * 256:a * HALF + (c + 1) * 256],
                                         start=True, stop=True)
                ins.then_inc(o_ready, 1)

            def two_batches(b):
                if b % 8 == 0:
                    return {0: lambda: att_scores(b), 3: lambda: att_scores(b + 1),
                            4: lambda: att_turn(b), 6: lambda: att_out(b),
                            7: lambda: att_scores(b + 2), 8: lambda: att_turn(b + 1)}
                steps = {0: lambda: (att_out(b - 1), att_scores(b + 1)), 2: lambda: att_turn(b),
                         4: lambda: att_out(b), 6: lambda: att_turn(b + 1)}
                steps.update({5: lambda: att_scores(b + 2)} if b % 8 < 6 else
                             {8: lambda: att_out(b + 1)})
                return steps

            for j in range(4):
                unit(h_hi_k, h_lo_k, 1, None, two_batches(2 * j))

            def o_ready_k(p):
                def ready(d, k):
                    if d == 0:
                        eng.wait_ge(h_ready, n("h", 4 * p + k + 1))
                return ready

            for j in range(4):
                unit(h_hi_k, h_lo_k, 2, o_ready_k(0), two_batches(8 + 2 * j))
            for _ in range(2):
                unit(lambda k: h_hi[:, 4 + k, :], lambda k: h_lo[:, 4 + k, :], 4, o_ready_k(1))
            last_two(lambda k: h_hi[:, 6 + k, :], lambda k: h_lo[:, 6 + k, :],
                     lambda k: eng.wait_ge(h_ready, n("h", 7 + k)))
            n.add("h", KT)
            mlp(False)
            square_sums(1)
            spread(1)

        @block.vector
        def _(eng):
            n = Counts()

            def split_lo(ahead=1):
                s = (n.n["unit"] + ahead) % 2
                eng.wait_ge(hi_split, n("unit", ahead + 1))
                eng.tensor_tensor(w_lo[:, s, :], raw[:, s, :], w_hi[:, s, :].bitcast(f32), ALU.subtract)\
                   .then_inc(lo_split, 1)

            def take(wait=True):
                if wait:
                    eng.wait_ge(acc_ready, n("tile", 1))
                s = n.n["tile"] % 2
                n.add("tile")
                n.add(f"set{s}")
                return s

            def ada_unit():
                i = n.n["ada"] % 4
                s, g = n.n["ada"] % 2, n.n["ada"] // 4 % 2
                eng.wait_ge(ada_in[s], n("ada", 8 * (2 - s), 8))
                dst = ada_acc[:, g, (i // 2) * ADA_N:(i // 2 + 1) * ADA_N]
                for k in range(ADA_KH):
                    kk = (i % 2) * ADA_KH + k
                    src = ada_raw[:, s, k * ADA_N:(k + 1) * ADA_N]
                    cv = cact[:, kk:kk + 1]
                    if kk == 0:
                        ins = eng.tensor_scalar(dst, src, cv, None, ALU.mult)
                    else:
                        eng.wait_ge(ada_step, ada_steps(k))
                        ins = eng.scalar_tensor_tensor(out=dst, in0=src, scalar=cv, in1=dst,
                                                       op0=ALU.mult, op1=ALU.add)
                    ins.then_inc(ada_step, 1)
                n.add("ada")

            def ada_steps(k):
                return n("ada", PRO_STEPS + k, ADA_KH)

            def mod_cols(at):
                ins = eng.tensor_tensor(modv[:, bass.ds(n("red", 16, 4), 4)], aux[:, at:at + 4],
                                        vecs[:, bass.ds(n("red", 16 + COLS["adab"], 4), 4)], ALU.add)
                n.add("red")
                return ins

            def stream(gate_at, d, c=None):
                s = take()
                w = half(c) if c is not None else slice(0, T)
                eng.scalar_tensor_tensor(out=x[:, d, w], in0=acc[s][:, w],
                                         scalar=modv[:, gate_at + d:gate_at + d + 1], in1=x[:, d, w],
                                         op0=ALU.mult, op1=ALU.add)\
                   .then_inc(acc_free[s], 1)

            def add_square(k, c=None):
                if k < 1:
                    return
                w = half(c) if c is not None else slice(0, T)
                eng.wait_ge(sq_done, n("sqadd", k + 1))
                if k == 1:
                    eng.tensor_tensor(sum_b[:, w], sq_b[0][:, w], sq_b[1][:, w], ALU.add)\
                       .then_inc(sq_added, 2)
                else:
                    eng.wait_ge(sq_added, n("sqadd", k))
                    eng.tensor_tensor(sum_b[:, w], sum_b[:, w], sq_b[k % 2][:, w], ALU.add)\
                       .then_inc(sq_added, 1)

            def mean(first=0, width=8, at=0):
                s = n.n["rs"] % 2
                n.add("aux")
                eng.wait_ge(aux_ready, n("aux"))
                eng.tensor_scalar(ms[:, s, first:first + width], aux[:, at:at + width], 1.0 / D, EPS,
                                  ALU.mult, ALU.add).then_inc(ms_ready, 1)

            def diagonal(first=0, width=8):
                s = n.n["rs"] % 2
                eng.wait_ge(rstd_ready, n("rs", 1))
                n.add("rs")
                eng.tensor_tensor(diag_b[:, first * P:(first + width) * P]
                                  .rearrange("p (c t) -> p c t", t=P),
                                  ident[:, :].rearrange("p (o t) -> p o t", o=1)
                                  .broadcast_to([P, width, P]),
                                  rstd[:, s, first:first + width].rearrange("p (c o) -> p c o", o=1)
                                  .broadcast_to([P, width, P]),
                                  ALU.mult).then_inc(aux_free, 1)
                n.add("aux")

            def rb_ready():
                eng.wait_ge(aux_free, n("aux"))

            def normed(steps):
                n.add("h", steps)
                n.add("xn", steps)

            def xn_step(i, c=None):
                k = i % KT
                w = half(c) if c is not None else slice(0, T)
                if k >= 2:
                    eng.wait_ge(hf_done, n("xn", i - 1))
                eng.tensor_tensor(xn_b[k % 2][:, w], x[:, k, w], rb_b[:, w], ALU.mult)\
                   .then_inc(xn_done, 1)

            def lo_step(i, c=None):
                k = i % KT
                w = half(c) if c is not None else slice(0, T)
                eng.wait_ge(hhi_done, n("h", i + 1))
                eng.tensor_tensor(h_lo[:, k, w], hf_b[k % 2][:, w], h_hi[:, k, w].bitcast(f32),
                                  ALU.subtract).then_inc(h_ready, 1)

            def last_two(gate_at, ada_too=False, columns=None, set_gains=None, between=None):
                for d in range(KT):
                    stream(gate_at, d, 0)
                    if d == 0:
                        split_lo()
                    add_square(d - 1, 0)
                    if d % 4 == 1 and ada_too:
                        ada_unit()
                add_square(KT - 1, 0)
                n.add("sqadd", KT)
                for d in range(KT):
                    if d == 5:
                        rb_ready()
                        between(0)
                    stream(gate_at, d, 1)
                    add_square(d - 1, 1)
                    if d == 0:
                        if columns:
                            columns()
                            eng.wait_ge(aux_free, n("aux"))
                        if set_gains:
                            set_gains()
                    if d == 1:
                        mean(0, 4)
                    if d == 3:
                        diagonal(0, 4)
                    if d >= 5:
                        between(d - 4)
                add_square(KT - 1, 1)
                n.add("sqadd", KT)
                n.add("unit", 2)

            def norm(gate_at, ada_too=False, columns=None, set_gains=None):
                def step(i):
                    if i == 3:
                        split_lo(3)
                    xn_step(i, 0)
                    if i:
                        lo_step(i - 1, 0)
                    if i == 0:
                        split_lo(2)

                last_two(gate_at, ada_too, columns, set_gains, step)
                step(4)
                mean(4, 4, HALF)
                step(5)
                step(6)
                diagonal(4, 4)
                step(7)
                lo_step(KT - 1, 0)
                rb_ready()
                for i in range(KT, 2 * KT):
                    xn_step(i, 1)
                    if i > KT:
                        lo_step(i - 1, 1)
                lo_step(2 * KT - 1, 1)
                normed(2 * KT)

            def gains(row, name, scale_at):
                eng.tensor_scalar(small[:, 4 + row, :], modv[:, scale_at:scale_at + 8], 1.0, None, ALU.add)\
                   .then_inc(gain_done, 1)
                eng.wait_ge(gain_done, 2 * row + 1)
                eng.tensor_tensor(gain[:, row, :], small[:, 4 + row, :], col(name, 0, 8), ALU.mult)\
                   .then_inc(gain_done, 1)

            eng.wait_ge(vecs_in, 16)
            eng.wait_ge(c_sig, 1)
            eng.tensor_tensor(cact[:, :], col("c", 0, 8), small[:, 0, :], ALU.mult).then_inc(c_act_done, 1)
            eng.tensor_tensor(small[:, 1, :], col("gamma", 0, 8), col("gamma", 0, 8), ALU.subtract)\
               .then_inc(lb_step, 1)
            eng.wait_ge(lb_exp, 1)
            eng.reciprocal(small[:, 3, :], small[:, 2, :]).then_inc(lb_step, 1)
            eng.wait_ge(lb_step, 2)
            eng.tensor_tensor(small[:, 3, :], small[:, 3, :], small[:, 2, :], ALU.mult).then_inc(lb_step, 1)
            eng.wait_ge(lb_step, 3)
            eng.tensor_tensor(lb[:, :], small[:, 3, :], small[:, 3, :], ALU.subtract).then_inc(lb_step, 1)
            eng.wait_ge(lb_step, 4)
            eng.tensor_scalar(lb[:, :], lb[:, :], 0.0, None, ALU.max).then_inc(lb_step, 1)
            eng.wait_ge(lb_step, 5)
            eng.tensor_scalar(omlb[:, :], lb[:, :], -1.0, 1.0, ALU.mult, ALU.add).then_inc(lb_step, 1)
            eng.wait_ge(c_act_done, 1)
            for j in range(0, ADA_FIRST, 2):
                eng.wait_ge(pro_in[j % 4], 16 * (j // 4 + 1))
                dst = pro_acc[:, j * ADA_N:(j + 1) * ADA_N]
                for k in range(KT):
                    src = pro_b[j % 4][:, k * ADA_N:(k + 1) * ADA_N]
                    if k == 0:
                        ins = eng.tensor_scalar(dst, src, cact[:, 0:1], None, ALU.mult)
                    else:
                        eng.wait_ge(ada_step, j // 2 * KT + k)
                        ins = eng.scalar_tensor_tensor(out=dst, in0=src, scalar=cact[:, k:k + 1],
                                                       in1=dst, op0=ALU.mult, op1=ALU.add)
                    ins.then_inc(ada_step, 1)
            for k in range(1, 4):
                add_square(k)
            n.add("aux")
            eng.wait_ge(aux_ready, n("aux"))
            eng.tensor_tensor(modv[:, 0:16], aux[:, 0:16], col("adab", 0, 16), ALU.add)\
               .then_inc(aux_free, 1)
            eng.wait_ge(aux_free, n("aux"))
            gains(0, "mix0", SC1)
            split_lo(0)
            add_square(4)
            add_square(5)
            split_lo(1)
            add_square(6)
            add_square(7)
            n.add("sqadd", KT)
            eng.wait_ge(const_in, 32)
            mean()
            diagonal()
            rb_ready()
            eng.wait_ge(masks_set, LEVELS + 1)
            for k in range(KT):
                xn_step(k)
                if k:
                    lo_step(k - 1)
            lo_step(KT - 1)
            normed(KT)

            def merge(j):
                if j == 1:
                    eng.wait_ge(lev_ready, n("head", 1, 8))
                    eng.tensor_tensor(q_b, q_b, f_b, ALU.mult).then_inc(merged, 1)
                    return
                L = 2 ** (j - 2)
                eng.wait_ge(lev_ready, n("head", j, 8))
                eng.wait_ge(merged, n("head", j - 1, 8))
                eng.wait_ge(lev_copied, n("head", j - 1, 8))
                fl = fprod(L).rearrange("p (b two) -> p b two", two=2)
                even, odd = fl[:, :, 0:1], fl[:, :, 1:2]
                nb = T // (2 * L)
                eng.tensor_tensor(fprod(2 * L).rearrange("p (b o) -> p b o", o=1), even, odd, ALU.mult)
                qr, kl = halves(q_b, L)[:, :, 1, :], halves(k_b, L)[:, :, 0, :]
                eng.tensor_tensor(qr, qr, even.broadcast_to([P, nb, L]), ALU.mult)
                eng.tensor_tensor(kl, kl, odd.broadcast_to([P, nb, L]), ALU.mult).then_inc(merged, 1)

            def keep(j):
                if j == 0:
                    eng.copy_predicated(a_b, masks[:, LEVELS * HALF:], lev[:, :]).then_inc(lev_copied, 1)
                    return
                L = 2 ** (j - 1)
                bank = (j - 1) % 2
                eng.copy_predicated(
                    halves(a_b, L)[:, :, 1, :],
                    masks[:, (j - 1) * HALF:j * HALF].rearrange("p (b l) -> p b l", l=L),
                    lev[:, bank * HALF:(bank + 1) * HALF].rearrange("p (b l) -> p b l", l=L))\
                   .then_inc(lev_copied, 1)

            def states():
                n.add("aux")
                eng.wait_ge(aux_ready, n("aux"))
                mod_cols(T - 4).then_inc(mod_done, 1)
                decay = fprod(P)
                eng.tensor_copy(s_b[:, 0:P], aux[:, 0:P]).then_inc(state_done, 1)
                last = NCH - 2
                for c in range(1, last + 1):
                    eng.wait_ge(state_done, n("head", c - last, last))
                    eng.scalar_tensor_tensor(out=s_b[:, c * P:(c + 1) * P],
                                                   in0=s_b[:, (c - 1) * P:c * P],
                                                   scalar=decay[:, c:c + 1],
                                                   in1=aux[:, c * P:(c + 1) * P],
                                                   op0=ALU.mult, op1=ALU.add)\
                       .then_inc(aux_free if c == last else state_done, 1)

            def norm_out():
                n.add("aux")
                s = n.n["rs"] % 2
                eng.wait_ge(osq_done, n("head"))
                eng.tensor_reduce(small[:, 15, :], osq_b.rearrange("p (c v) -> p c v", v=P), AX.X, ALU.add)\
                   .then_inc(osq_summed, 1)
                eng.wait_ge(osq_summed, n("head"))
                eng.tensor_scalar(ms[:, s, :], small[:, 15, :], 1.0 / P, EPS, ALU.mult, ALU.add)\
                   .then_inc(ms_ready, 1)
                eng.wait_ge(rstd_ready, n("rs", 1))
                n.add("rs")
                eng.tensor_tensor(on_b.rearrange("p (c v) -> p c v", v=P),
                                  aux[:, :].rearrange("p (c v) -> p c v", v=P),
                                  rstd[:, s, :].rearrange("p (c o) -> p c o", o=1).broadcast_to([P, NCH, P]),
                                  ALU.mult).then_inc(aux_free, 1)

            def gate_out():
                n.add("aux")
                eng.wait_ge(acc_free[1], n("set1"))
                eng.wait_ge(aux_ready, n("aux"))
                eng.scalar_tensor_tensor(out=g_b, in0=aux[:, :], scalar=col("gnorm"), in1=g_b,
                                         op0=ALU.mult, op1=ALU.mult)\
                   .then_inc(aux_free, 1)

            def part_lo():
                e = (n.n["head"] + 1) % 2
                eng.wait_ge(ohi_done, n("head"))
                eng.tensor_tensor(o_lo[:, e, :], g_b, o_hi[:, e, :].bitcast(f32), ALU.subtract)\
                   .then_inc(o_split, 1)

            def slot_f(tail):
                if tail:
                    split_lo()
                ada_unit()
                if tail:
                    n.add("aux")
                    states()
                s = take()
                if not tail:
                    split_lo(2)
                hd = n("head")
                eng.wait_ge(f_raw, n("head", 1))
                eng.tensor_scalar(f_b, f_b, omlb[:, bass.ds(hd, 1)], lb[:, bass.ds(hd, 1)],
                                  ALU.mult, ALU.add).then_inc(gates_done, 1)
                eng.wait_ge(acc_free[s], n(f"set{s}"))
                eng.tensor_scalar(k_b, k_b, omlb[:, bass.ds(hd, 1)], None, ALU.mult)\
                   .then_inc(gates_done, 1)
                n.add("unit")

            def slot_q(tail):
                if tail:
                    split_lo()
                ada_unit()
                if tail:
                    norm_out()
                s = take()
                eng.wait_ge(q_sig, n("head", 1))
                eng.tensor_tensor(q_b, q_b, acc[s][:, :], ALU.mult)\
                   .then_inc(acc_free[s], 1)
                n.add("unit")

            def slot_i(tail):
                split_lo()
                ada_unit()
                if tail:
                    gate_out()
                else:
                    eng.wait_ge(a_zero, 1)
                eng.wait_ge(gates_done, n("head", 2, 2))
                eng.wait_ge(acc_free[1], n("set1"))
                for j in range(3):
                    merge(j + 1)
                    keep(j)
                    if tail and j == 0:
                        part_lo()
                take(False)
                n.add("unit")

            def out_units():
                for un in range(2):
                    for d in range(4):
                        stream(G1, 4 * un + d)
                        if d == 0:
                            split_lo()
                    n.add("unit")

            def slot_g():
                split_lo()
                ada_unit()
                n.add("aux")
                for j in range(3, 8):
                    merge(j + 1)
                    keep(j)
                s = take()
                eng.wait_ge(g_sig, n("head", 1))
                eng.tensor_tensor(g_b, g_b, acc[s][:, :], ALU.mult)\
                   .then_inc(acc_free[s], 1)
                n.add("unit")
                n.add("head")

            def pair(first):
                for e in range(2):
                    tail = not (first and e == 0)
                    slot_f(tail)
                    slot_q(tail)
                    slot_i(tail)
                    if e == 0 and not first:
                        out_units()
                    slot_g()

            pair(True)
            with eng.Fori(0, 3) as i:
                n.enter(i, HG_PAIR)
                pair(False)
                n.leave(3)
            n.add("aux")
            states()
            norm_out()
            gate_out()
            part_lo()

            def mlp_0_gains():
                eng.wait_ge(mod_done, HEADS)
                gains(1, "mlp0", SC2)

            norm(G1, set_gains=mlp_0_gains)

            def mlp(ada_too, gate_at, end):
                def hidden_lo():
                    j, par = n.n["hid"] % 2, n.n["hid"] // 2 % 2
                    eng.wait_ge(hidhi_done, n("hid", 1))
                    eng.tensor_tensor(hid_lo[:, par, j, :], relu_b[j],
                                      hid_hi[:, par, j, :].bitcast(f32), ALU.subtract)\
                       .then_inc(hid_done, 1)
                    n.add("hid")

                def first(g):
                    for un in range(GROUP):
                        if g:
                            split_lo()
                        if ada_too:
                            ada_unit()
                        if g == 0 and un == 0:
                            split_lo(2)
                        take(False)
                        if g == 0 or un == 0:
                            hidden_lo()
                        n.add("unit")

                def second():
                    for un in range(2):
                        for d in range(4):
                            stream(gate_at, 4 * un + d)
                            if un == 0 and d == 0:
                                hidden_lo()
                            if d == 1 - un:
                                split_lo()
                            if d == 2 - un and ada_too:
                                ada_unit()
                            if un == 0 and d == 2 and ada_too:
                                group_cols()
                        n.add("unit")

                def group_cols():
                    n.add("aux")
                    eng.wait_ge(aux_ready, n("aux"))
                    mod_cols(0).then_inc(aux_free, 1)

                first(0)
                first(1)
                second()
                with eng.Fori(0, MLP_LOOP) as i:
                    n.enter(i, MLP_TWO_ADA if ada_too else MLP_TWO)
                    for g in (1, 2):
                        first(g + 1)
                        second()
                    n.leave(MLP_LOOP)
                end(group_cols)

            def attention_gains():
                gains(2, "kvn", KSC)
                gains(3, "mix1", SC1B)

            mlp(True, G2, lambda columns: norm(G2, True, columns, attention_gains))

            for j in range(4):
                if j == 0:
                    split_lo(2)
                if j > 1:
                    split_lo()
                if j == 3:
                    for k in range(5):
                        xn_step(k)
                        if k:
                            lo_step(k - 1)
                take(False)
                n.add("unit")
            split_lo()
            for k in range(5, KT):
                xn_step(k)
                lo_step(k - 1)
            lo_step(KT - 1)
            normed(KT)
            n.add("aux", 4)

            def blocks(buf):
                return buf.rearrange("p (j n) -> p j n", n=P)

            def maxima(b):
                eng.wait_ge(s_ready, b + 1)
                if b % 8 == 0:
                    for a in range(2):
                        for c in range(2):
                            j = 4 * a + 2 * c
                            w = P if c else QCH
                            ins = eng.tensor_reduce(smx[:, 0, j:j + 2],
                                                    blocks(lev[:, :])[:, j:j + 2, 0:w], AX.X, ALU.max)
                    ge(eng, t_ready, b)
                    for a in range(2):
                        zero = eng.memset(blocks(p_b)[:, 4 * a:4 * a + 2, QCH:P], 0.0)
                    zero.then_inc(pmask, 1)
                else:
                    ins = eng.tensor_reduce(smx[:, 0, :], blocks(lev[:, :]), AX.X, ALU.max)
                ins.then_inc(sm_step, 1)
                sink = col("sink", 8 * (b // 8), 8)
                eng.wait_ge(sm_step, 7 * b + 1)
                eng.scalar_tensor_tensor(out=smx[:, 1, :], in0=smx[:, 0, :], scalar=SCORE_SCALE,
                                         in1=sink, op0=ALU.mult, op1=ALU.max).then_inc(sm_step, 1)
                eng.wait_ge(sm_step, 7 * b + 2)
                eng.tensor_scalar(smx[:, 2, :], smx[:, 1, :], -1.0, None, ALU.mult).then_inc(sm_step, 1)
                eng.tensor_tensor(smx[:, 3, :], sink, smx[:, 1, :], ALU.subtract).then_inc(sm_step, 1)

            def normalise(b):
                eng.wait_ge(p_exp, b + 1)
                eng.tensor_reduce(smx[:, 5, :], blocks(p_b), AX.X, ALU.add).then_inc(sm_step, 1)
                eng.wait_ge(snk_exp, b + 1)
                eng.wait_ge(sm_step, 7 * b + 5)
                eng.tensor_tensor(smx[:, 5, :], smx[:, 5, :], smx[:, 4, :], ALU.add).then_inc(sm_step, 1)
                eng.wait_ge(sm_step, 7 * b + 6)
                eng.reciprocal(smx[:, 1, :], smx[:, 5, :]).then_inc(sm_step, 1)
                eng.wait_ge(sm_step, 7 * b + 7)
                eng.tensor_tensor(blocks(p_b), blocks(p_b),
                                  smx[:, 1, :].rearrange("p (j o) -> p j o", o=1).broadcast_to([P, 8, P]),
                                  ALU.mult).then_inc(p_done, 1)

            def heads_out(b):
                p, m = b // 8, b % 8
                eng.wait_ge(o_ready, b + 1)
                eng.tensor_copy(qT[:, p, 2 * m:2 * m + 2, :, :].rearrange("p c g q -> p (c g q)"),
                                aux[:, 0:HALF]).then_inc(att_done, 1)

            def o_lo_part(p):
                for k in range(4 * p, 4 * p + 4):
                    eng.wait_ge(hhi_done, n("h", k + 1))
                    eng.tensor_tensor(h_lo[:, k, :].rearrange("p (n q) -> p n q", q=QCH),
                                      qT[:, p, :, k % 4, :],
                                      h_hi[:, k, :].bitcast(f32).rearrange("p (n q) -> p n q", q=QCH),
                                      ALU.subtract).then_inc(h_ready, 1)

            def batches(b, early=None, late=None):
                if b % 8 == 0:
                    split_lo()
                    maxima(b)
                else:
                    heads_out(b - 1)
                normalise(b)
                if early is not None:
                    stream(G1B, early)
                maxima(b + 1)
                if b % 8:
                    split_lo()
                heads_out(b)
                if late is not None:
                    stream(G1B, late)
                normalise(b + 1)
                if b % 8 < 6:
                    maxima(b + 2)
                else:
                    heads_out(b + 1)

            for j in range(4):
                if j:
                    split_lo()
                take(False)
                n.add("unit")
            for j in range(4):
                batches(2 * j)
                take(False)
                n.add("unit")
            o_lo_part(0)
            for j in range(4):
                batches(8 + 2 * j, 2 * j - 1 if j else None, 2 * j)
                n.add("unit")
            stream(G1B, KT - 1)
            o_lo_part(1)
            for un in range(2):
                for d in range(4):
                    stream(G1B, 4 * un + d)
                    if d == 0:
                        split_lo()
                n.add("unit")
            n.add("h", KT)
            norm(G1B, set_gains=lambda: gains(4, "mlp1", SC2B))

            def out_step(i, c=0):
                k = i % KT
                eng.scalar_tensor_tensor(out=out_b[k][:, half(c)], in0=x[:, k, half(c)],
                                         scalar=col("fin", k), in1=rb_b[:, half(c)],
                                         op0=ALU.mult, op1=ALU.mult).then_inc(fin_done, 1)

            def finish(_):
                last_two(G2B, between=out_step)
                mean(4, 4, HALF)
                for k in range(4, 6):
                    out_step(k)
                diagonal(4, 4)
                for k in range(6, KT):
                    out_step(k)
                rb_ready()
                for k in range(KT):
                    out_step(k, 1)

            mlp(False, G2B, finish)



def kernel(**inputs):
    import numpy as np
    import concourse.bacc as bacc
    from concourse.bass_utils import run_bass_kernel_spmd

    a = {k: np.asarray(v) for k, v in inputs.items()}
    f32 = mybir.dt.float32

    def square_units(w):
        k, m = w.shape
        return w.reshape(KT, P, m // P, P).transpose(2, 1, 0, 3).reshape(m // P, P, UNIT)

    def wide_units(w, kn):
        r, m = w.shape
        wide = UNIT // kn
        return w.reshape(r // (kn * P), kn, P, m // wide, wide).transpose(0, 3, 2, 1, 4)\
                .reshape(-1, P, UNIT)

    def by_pairs(w):
        return w.reshape((2, 2, 4, 64) + w.shape[1:]).transpose((0, 2, 1, 3) + tuple(range(4, 3 + w.ndim)))\
                .reshape(w.shape)

    w_in, w_out = a["hg_w_in"][0], a["hg_w_out"][0]
    uq, uf, ui, ug = (square_units(w_in[:, i * D:(i + 1) * D]) for i in range(4))
    uo = wide_units(w_out, 2)
    units = []
    for pr in range(HEADS // 2):
        for e in range(2):
            hd = 2 * pr + e
            units += [uf[hd], uq[hd], ui[hd]]
            if e == 0 and pr:
                units += [uo[2 * pr - 2], uo[2 * pr - 1]]
            units += [ug[hd]]
    units += [uo[6], uo[7]]

    def mlp_units(l):
        u1, u2 = square_units(a["mlp_w1"][l]), wide_units(a["mlp_w2"][l], GROUP)
        out = [u1[0], u1[1]]
        for g in range(NGROUPS):
            if g + 1 < NGROUPS:
                out += [u1[2 * g + 2], u1[2 * g + 3]]
            out += [u2[2 * g], u2[2 * g + 1]]
        return out

    units += mlp_units(0)
    units += list(square_units(a["kv_w"]))
    units += list(square_units(by_pairs(a["sw_w_q"][0].T).T))
    w_o = by_pairs(a["sw_w_o"][0])
    units += list(wide_units(w_o[0:D // 2], 4)) + list(wide_units(w_o[D // 2:], 2))
    units += mlp_units(1)
    weights = np.stack(units)
    assert weights.shape == (N_UNITS, P, UNIT)

    ada = np.concatenate([a["ada_w"][0], a["kv_ada_w"], a["ada_w"][1]], axis=1)
    ada = ada.reshape(2, ADA_KH, P, ADA_CHUNKS, ADA_N).transpose(3, 0, 2, 1, 4)\
             .reshape(2 * ADA_CHUNKS, P, ADA_KH * ADA_N)

    def columns(v):
        return v.reshape(-1, P).T

    sinks = a["sw_sinks"][0].reshape(2, 2, 2, 2)
    sink = np.empty((P, 2, 2, 2, 2), sinks.dtype)
    for g2 in range(2):
        sink[64 * g2:64 * g2 + 64] = sinks[None, :, :, None, :, g2]
    parts = dict(c=columns(a["c"][0]), mix0=columns(a["norm_mix"][0]), mix1=columns(a["norm_mix"][1]),
                 mlp0=columns(a["norm_mlp"][0]), mlp1=columns(a["norm_mlp"][1]),
                 kvn=columns(a["kv_norm"]), fin=columns(a["final_norm"]),
                 gnorm=columns(a["hg_g_norm"][0]), gamma=columns(a["hg_lb_gamma"][0]),
                 kvb=columns(a["kv_b"]), bq=columns(by_pairs(a["sw_b_q"][0])),
                 sink=sink.reshape(P, 16),
                 adab=columns(np.concatenate([a["ada_b"][0], a["kv_ada_b"], a["ada_b"][1]])))
    cols = np.ascontiguousarray(np.concatenate([parts[k] for k in COLS], axis=1))

    key, query = np.arange(P)[:, None], np.arange(P)[None, :]
    masks = []
    for j in range(LEVELS):
        L = 2 ** j
        pairs = (key // (2 * L) == query // (2 * L)) & (key // L % 2 == 0)
        masks.append(pairs[:, query[0] // L % 2 == 1])
    masks = np.concatenate(masks + [key == query], axis=1).astype(np.float32)

    arrays = {
        "xT": np.ascontiguousarray(a["x"][0].T).reshape(KT, P, T),
        "weights": weights, "ada": np.ascontiguousarray(ada), "cols": cols,
        "ident": np.eye(P, dtype=np.float32), "masks": masks,
    }
    nc = bacc.Bacc("TRN2", target_bir_lowering=False, num_devices=1)
    aps = [nc.dram_tensor("in_" + k, v.shape, mybir.dt.from_np(v.dtype), kind="ExternalInput").ap()
           for k, v in arrays.items()]
    out = nc.dram_tensor("outT", (KT, P, T), f32, kind="ExternalOutput").ap()
    build(nc, *aps, out)
    r = run_bass_kernel_spmd(nc, [{"in_" + k: v for k, v in arrays.items()}], core_ids=[0])
    return np.ascontiguousarray(r.results[0]["outT"].reshape(D, T).T)[None]
```
